# Optimizing a Trainium2 kernel written in Bass

```python
import jax, jax.numpy as jnp
from jax import lax
import numpy as np
import math

D_MODEL = 2048
BATCH = 1
SEQ = 256
DEPTH = 1

N_META = 16
CONV_CH = D_MODEL
CONV_WIDTH = 31
GLA_HEADS = 4
GLA_DK = D_MODEL // 2 // GLA_HEADS
GLA_DV = D_MODEL // GLA_HEADS
GLA_GATE_RANK = 16
GLA_TAU = 16.0
GLA_CHUNK = 64
PEER_HEADS = 8
PEER_NKEYS = 128
PEER_N = PEER_NKEYS * PEER_NKEYS
PEER_DK = 256
PEER_TOPK = 16
PEER_TOKEN_BLOCK = 128
EPS = 1e-6

COL_CONV = 2 * CONV_CH
COL_Q = GLA_HEADS * GLA_DK
COL_K = GLA_HEADS * GLA_DK
COL_V = GLA_HEADS * GLA_DV
COL_R = GLA_HEADS * GLA_DV
COL_A = GLA_GATE_RANK
COL_MERGE = 2 * D_MODEL
COL_TOTAL = COL_CONV + COL_Q + COL_K + COL_V + COL_R + COL_A + COL_MERGE


def _rmsnorm(x, g):
    xf = x.astype(jnp.float32)
    y = xf * lax.rsqrt(jnp.mean(xf * xf, axis=-1, keepdims=True) + EPS)
    return (y * g.astype(jnp.float32)).astype(x.dtype)

def _conv_module(a, conv_w, conv_b, ln_g, ln_b, w_out):
    h = a[..., :CONV_CH] * jax.nn.sigmoid(a[..., CONV_CH:])
    hp = jnp.pad(h, ((0, 0), (CONV_WIDTH - 1, 0), (0, 0)))
    h = lax.conv_general_dilated(hp, conv_w[:, None, :], window_strides=(1,), padding='VALID',
                                 dimension_numbers=('NWC', 'WIO', 'NWC'),
                                 feature_group_count=CONV_CH) + conv_b
    hf = h.astype(jnp.float32)
    mu = jnp.mean(hf, axis=-1, keepdims=True)
    var = jnp.mean(jnp.square(hf - mu), axis=-1, keepdims=True)
    hf = (hf - mu) * lax.rsqrt(var + EPS) * ln_g.astype(jnp.float32) + ln_b.astype(jnp.float32)
    h = jax.nn.silu(hf).astype(a.dtype)
    return h @ w_out

def _gla_branch(q, k, v, r, a_low, w_a2, b_a, norm_g, w_o):
    B, L, _ = q.shape
    H, dk, dv, C = GLA_HEADS, GLA_DK, GLA_DV, GLA_CHUNK
    pad = C - N_META
    log_a = jax.nn.log_sigmoid((a_low @ w_a2 + b_a).astype(jnp.float32)) / GLA_TAU

    def to_chunks(t, d):
        t = jnp.pad(t.astype(jnp.float32), ((0, 0), (pad, 0), (0, 0)))
        n = t.shape[1] // C
        return t.reshape(B, n, C, H, d).transpose(1, 0, 3, 2, 4)

    qc = to_chunks(q, dk) * (dk ** -0.5)
    kc = to_chunks(k, dk)
    vc = to_chunks(v, dv)
    gc = to_chunks(log_a, dk)
    mask = jnp.tril(jnp.ones((C, C), dtype=bool))[None, None, :, :, None]

    def step(S, inp):
        qb, kb, vb, gb = inp
        b = jnp.cumsum(gb, axis=2)
        o_inter = jnp.einsum('bhcd,bhde->bhce', qb * jnp.exp(b), S)
        diff = b[:, :, :, None, :] - b[:, :, None, :, :]
        decay = jnp.exp(jnp.where(mask, diff, -jnp.inf))
        att = jnp.einsum('bhid,bhjd,bhijd->bhij', qb, kb, decay)
        o_intra = jnp.einsum('bhij,bhje->bhie', att, vb)
        b_last = b[:, :, -1:, :]
        S_new = jnp.exp(b_last[:, :, 0, :])[..., None] * S + \
            jnp.einsum('bhjd,bhje->bhde', kb * jnp.exp(b_last - b), vb)
        return S_new, o_inter + o_intra

    S0 = jnp.zeros((B, H, dk, dv), jnp.float32)
    _, o = lax.scan(step, S0, (qc, kc, vc, gc))
    n = o.shape[0]
    o = o.transpose(1, 0, 3, 2, 4).reshape(B, n * C, H, dv)[:, pad:]
    o = o * lax.rsqrt(jnp.mean(o * o, axis=-1, keepdims=True) + EPS)
    o = o * norm_g.astype(jnp.float32).reshape(H, dv)
    o = o * jax.nn.silu(r.astype(jnp.float32)).reshape(B, L, H, dv)
    return o.reshape(B, L, H * dv).astype(w_o.dtype) @ w_o

def _peer(xn, wq, k1, k2, U, V):
    B, L, D = xn.shape
    PH, NK, K, half = PEER_HEADS, PEER_NKEYS, PEER_TOPK, PEER_DK // 2
    q = (xn @ wq).astype(jnp.float32).reshape(B, L, PH, PEER_DK)
    s1 = jnp.einsum('blhd,hnd->blhn', q[..., :half], k1.astype(jnp.float32))
    s2 = jnp.einsum('blhd,hnd->blhn', q[..., half:], k2.astype(jnp.float32))
    v1, i1 = lax.top_k(s1, K)
    v2, i2 = lax.top_k(s2, K)
    cand = (v1[..., :, None] + v2[..., None, :]).reshape(B, L, PH, K * K)
    cidx = (i1[..., :, None] * NK + i2[..., None, :]).reshape(B, L, PH, K * K)
    top_s, pos = lax.top_k(cand, K)
    idx = jnp.take_along_axis(cidx, pos, axis=-1)
    gate = jax.nn.softmax(top_s, axis=-1)

    T = B * L
    TB = PEER_TOKEN_BLOCK
    nblk = -(-T // TB)
    padT = nblk * TB - T
    xt = jnp.pad(xn.reshape(T, D), ((0, padT), (0, 0))).reshape(nblk, TB, D)
    it = jnp.pad(idx.reshape(T, PH, K), ((0, padT), (0, 0), (0, 0))).reshape(nblk, TB, PH, K)
    gt = jnp.pad(gate.reshape(T, PH, K), ((0, padT), (0, 0), (0, 0))).reshape(nblk, TB, PH, K)

    def block(args):
        xb, ib, gb = args
        u = U[ib]
        h = jax.nn.gelu(jnp.einsum('thkd,td->thk', u, xb).astype(jnp.float32), approximate=False)
        w = (gb * h).astype(xb.dtype)
        return jnp.einsum('thk,thkd->td', w, V[ib])

    y = lax.map(block, (xt, it, gt)).reshape(nblk * TB, D)[:T]
    return y.reshape(B, L, D).astype(xn.dtype)

def first_inputs(seed: int = 0) -> dict:
    key = jax.random.key(seed)
    ks = jax.random.split(key, 24)

    def nrm(k, shape, scale):
        return jax.random.normal(k, shape, jnp.float32) * scale

    Dp = DEPTH
    return {
        "x": nrm(ks[0], (BATCH, SEQ, D_MODEL), 1.0),
        "meta_tokens": nrm(ks[1], (N_META, D_MODEL), 1.0),
        "norm1_g": 1.0 + nrm(ks[2], (Dp, D_MODEL), 0.02),
        "w_in": nrm(ks[3], (Dp, D_MODEL, COL_TOTAL), D_MODEL ** -0.5),
        "w_alpha2": nrm(ks[4], (Dp, GLA_GATE_RANK, GLA_HEADS * GLA_DK), GLA_GATE_RANK ** -0.5),
        "b_alpha": nrm(ks[5], (Dp, GLA_HEADS * GLA_DK), 0.1),
        "conv_w": nrm(ks[6], (Dp, CONV_WIDTH, CONV_CH), CONV_WIDTH ** -0.5),
        "conv_b": nrm(ks[7], (Dp, CONV_CH), 0.02),
        "conv_ln_g": 1.0 + nrm(ks[8], (Dp, CONV_CH), 0.02),
        "conv_ln_b": nrm(ks[9], (Dp, CONV_CH), 0.02),
        "w_conv_out": nrm(ks[10], (Dp, CONV_CH, D_MODEL), CONV_CH ** -0.5),
        "gla_norm_g": 1.0 + nrm(ks[11], (Dp, GLA_HEADS * GLA_DV), 0.02),
        "w_gla_out": nrm(ks[12], (Dp, GLA_HEADS * GLA_DV, D_MODEL), (GLA_HEADS * GLA_DV) ** -0.5),
        "w_out": nrm(ks[13], (Dp, D_MODEL, D_MODEL), D_MODEL ** -0.5),
        "norm2_g": 1.0 + nrm(ks[14], (Dp, D_MODEL), 0.02),
        "peer_wq": nrm(ks[15], (Dp, D_MODEL, PEER_HEADS * PEER_DK), D_MODEL ** -0.5),
        "peer_k1": nrm(ks[16], (Dp, PEER_HEADS, PEER_NKEYS, PEER_DK // 2), (PEER_DK // 2) ** -0.5),
        "peer_k2": nrm(ks[17], (Dp, PEER_HEADS, PEER_NKEYS, PEER_DK // 2), (PEER_DK // 2) ** -0.5),
        "peer_u": nrm(ks[18], (Dp, PEER_N, D_MODEL), D_MODEL ** -0.5),
        "peer_v": nrm(ks[19], (Dp, PEER_N, D_MODEL), PEER_HEADS ** -0.5),
        "normf_g": 1.0 + nrm(ks[20], (D_MODEL,), 0.02),
    }

def first_block(x, meta_tokens, norm1_g, w_in, w_alpha2, b_alpha, conv_w, conv_b, conv_ln_g, conv_ln_b,
              w_conv_out, gla_norm_g, w_gla_out, w_out, norm2_g, peer_wq, peer_k1, peer_k2,
              peer_u, peer_v, normf_g):
    B = x.shape[0]
    meta = jnp.broadcast_to(meta_tokens[None].astype(x.dtype), (B, N_META, D_MODEL))
    h = jnp.concatenate([meta, x], axis=1)
    offs = [COL_CONV, COL_Q, COL_K, COL_V, COL_R, COL_A]
    cuts = [int(c) for c in np.cumsum(offs)]
    for l in range(DEPTH):
        xn = _rmsnorm(h, norm1_g[l])
        proj = xn @ w_in[l]
        a_conv, q, k, v, r, a_low, g_merge = jnp.split(proj, cuts, axis=-1)
        y_conv = _conv_module(a_conv, conv_w[l], conv_b[l], conv_ln_g[l], conv_ln_b[l], w_conv_out[l])
        y_gla = _gla_branch(q, k, v, r, a_low, w_alpha2[l], b_alpha[l], gla_norm_g[l], w_gla_out[l])
        gates = jax.nn.sigmoid(g_merge.astype(jnp.float32))
        mixed = gates[..., :D_MODEL] * y_conv.astype(jnp.float32) + gates[..., D_MODEL:] * y_gla.astype(jnp.float32)
        h = h + mixed.astype(h.dtype) @ w_out[l]
        h = h + _peer(_rmsnorm(h, norm2_g[l]), peer_wq[l], peer_k1[l], peer_k2[l], peer_u[l], peer_v[l])
    return _rmsnorm(h, normf_g)[:, N_META:]


N_MEM = 256
N_MIXERS = 2
EXPAND = 2
INNER = EXPAND * D_MODEL
XA_HEADS = 4
XA_WIDTH = INNER // 4
XA_DIM = XA_WIDTH // XA_HEADS
MIX_WIDTH = INNER - XA_WIDTH
DN_HEAD_DIM = 128
DN_V_HEADS = MIX_WIDTH // DN_HEAD_DIM
DN_QK_HEADS = DN_V_HEADS // 2
DN_QK_WIDTH = DN_QK_HEADS * DN_HEAD_DIM
DN_CONV = 4
DN_CHUNK = 64
DN_MIX_COLS = 2 * DN_QK_WIDTH + MIX_WIDTH + 2 * DN_V_HEADS
DN_PROJ = DN_MIX_COLS + XA_WIDTH + INNER
SB_HEAD_DIM = 128
SB_HEADS = MIX_WIDTH // SB_HEAD_DIM
SB_BLOCK = 128
SB_MIX_COLS = 3 * MIX_WIDTH
SB_PROJ = SB_MIX_COLS + XA_WIDTH + INNER


def rms_norm(x, g):
    xf = x.astype(jnp.float32)
    y = xf * lax.rsqrt(jnp.mean(xf * xf, axis=-1, keepdims=True) + EPS)
    return (y * g.astype(jnp.float32)).astype(x.dtype)

def l2_norm(x):
    xf = x.astype(jnp.float32)
    return (xf * lax.rsqrt(jnp.sum(xf * xf, axis=-1, keepdims=True) + EPS)).astype(x.dtype)

def causal_depthwise_conv(x, w):
    c = x.shape[-1]
    return lax.conv_general_dilated(
        x, w[:, None, :].astype(x.dtype), window_strides=(1,),
        padding=((w.shape[0] - 1, 0),), dimension_numbers=("NWC", "WIO", "NWC"),
        feature_group_count=c)

def gated_delta_rule(q, k, v, g, beta):
    f32 = jnp.float32
    B, H, S, dk = q.shape
    dv = v.shape[-1]
    C, N = DN_CHUNK, S // DN_CHUNK
    q, k, v = (t.astype(f32).reshape(B, H, N, C, t.shape[-1]) for t in (q, k, v))
    g = g.astype(f32).reshape(B, H, N, C)
    beta = beta.astype(f32).reshape(B, H, N, C)
    gc = jnp.cumsum(g, axis=-1)
    idx = jnp.arange(C)
    incl = idx[:, None] >= idx[None, :]
    strict = idx[:, None] > idx[None, :]
    decay = jnp.exp(jnp.where(incl, gc[..., :, None] - gc[..., None, :], -jnp.inf))
    kk = jnp.einsum("bhncd,bhnjd->bhncj", k, k)
    m = jnp.where(strict, beta[..., :, None] * kk * decay, 0.0) + jnp.eye(C, dtype=f32)
    rhs = jnp.concatenate([v * beta[..., None], k * (beta * jnp.exp(gc))[..., None]], axis=-1)
    sol = lax.linalg.triangular_solve(m, rhs, left_side=True, lower=True, unit_diagonal=True)
    u0, w = sol[..., :dv], sol[..., dv:]
    qk = jnp.einsum("bhncd,bhnjd->bhncj", q, k) * decay
    q_dec = q * jnp.exp(gc)[..., None]
    k_dec = k * jnp.exp(gc[..., -1:] - gc)[..., None]
    chunk_decay = jnp.exp(gc[..., -1])

    def step(state, inp):
        u0_c, w_c, qk_c, qd_c, kd_c, cd_c = inp
        u = u0_c - jnp.einsum("bhcd,bhde->bhce", w_c, state)
        o = jnp.einsum("bhcd,bhde->bhce", qd_c, state) + jnp.einsum("bhcj,bhje->bhce", qk_c, u)
        state = cd_c[..., None, None] * state + jnp.einsum("bhcd,bhce->bhde", kd_c, u)
        return state, o

    xs = tuple(jnp.moveaxis(t, 2, 0) for t in (u0, w, qk, q_dec, k_dec, chunk_decay))
    _, o = lax.scan(step, jnp.zeros((B, H, dk, dv), f32), xs)
    return jnp.moveaxis(o, 0, 2).reshape(B, H, S, dv)

def deltanet_branch(p, conv_w, a_log, dt_bias, out_g):
    B, S, _ = p.shape
    c_qkv = 2 * DN_QK_WIDTH + MIX_WIDTH
    qkv = jax.nn.silu(causal_depthwise_conv(p[..., :c_qkv], conv_w))
    q = qkv[..., :DN_QK_WIDTH].reshape(B, S, DN_QK_HEADS, DN_HEAD_DIM)
    k = qkv[..., DN_QK_WIDTH:2 * DN_QK_WIDTH].reshape(B, S, DN_QK_HEADS, DN_HEAD_DIM)
    v = qkv[..., 2 * DN_QK_WIDTH:].reshape(B, S, DN_V_HEADS, DN_HEAD_DIM)
    a = p[..., c_qkv:c_qkv + DN_V_HEADS].astype(jnp.float32)
    b = p[..., c_qkv + DN_V_HEADS:].astype(jnp.float32)
    rep = DN_V_HEADS // DN_QK_HEADS
    q = jnp.repeat(l2_norm(q), rep, axis=2) * DN_HEAD_DIM ** -0.5
    k = jnp.repeat(l2_norm(k), rep, axis=2)
    g = -jnp.exp(a_log.astype(jnp.float32)) * jax.nn.softplus(a + dt_bias.astype(jnp.float32))
    beta = jax.nn.sigmoid(b)
    o = gated_delta_rule(q.transpose(0, 2, 1, 3), k.transpose(0, 2, 1, 3), v.transpose(0, 2, 1, 3),
                         g.transpose(0, 2, 1), beta.transpose(0, 2, 1))
    o = rms_norm(o.astype(p.dtype), out_g)
    return o.transpose(0, 2, 1, 3).reshape(B, S, MIX_WIDTH)

def stick_breaking_attention(q, k, v):
    B, H, S, d = q.shape
    scale = d ** -0.5
    outs = []
    for blk in range(S // SB_BLOCK):
        q0 = blk * SB_BLOCK
        kv_len = q0 + SB_BLOCK
        qb = q[:, :, q0:kv_len]
        kb, vb = k[:, :, :kv_len], v[:, :, :kv_len]
        z = jnp.einsum("bhtd,bhsd->bhts", qb, kb).astype(jnp.float32) * scale
        t_pos = q0 + jnp.arange(SB_BLOCK)
        s_pos = jnp.arange(kv_len)
        mask = s_pos[None, :] < t_pos[:, None]
        log_rest = jnp.where(mask, jax.nn.log_sigmoid(-z), 0.0)
        later = lax.cumsum(log_rest, axis=3, reverse=True) - log_rest
        wts = jnp.where(mask, jnp.exp(jax.nn.log_sigmoid(z) + later), 0.0)
        outs.append(jnp.einsum("bhts,bhsd->bhtd", wts.astype(v.dtype), vb))
    return jnp.concatenate(outs, axis=2)

def stick_breaking_branch(p, qn_g, kn_g):
    B, S, _ = p.shape
    q, k, v = (t.reshape(B, S, SB_HEADS, SB_HEAD_DIM) for t in jnp.split(p, 3, axis=-1))
    q, k = rms_norm(q, qn_g), rms_norm(k, kn_g)
    o = stick_breaking_attention(q.transpose(0, 2, 1, 3), k.transpose(0, 2, 1, 3), v.transpose(0, 2, 1, 3))
    return o.transpose(0, 2, 1, 3).reshape(B, S, MIX_WIDTH)

def memory_cross_attention(xq, mem_n, w_kv, qn_g, kn_g):
    B, S, _ = xq.shape
    q = rms_norm(xq.reshape(B, S, XA_HEADS, XA_DIM), qn_g)
    kv = jnp.einsum("bmd,de->bme", mem_n, w_kv)
    k = rms_norm(kv[..., :XA_WIDTH].reshape(B, -1, XA_HEADS, XA_DIM), kn_g)
    v = kv[..., XA_WIDTH:].reshape(B, -1, XA_HEADS, XA_DIM)
    s = jnp.einsum("bthd,bmhd->bhtm", q, k).astype(jnp.float32) * XA_DIM ** -0.5
    p = jax.nn.softmax(s, axis=-1).astype(v.dtype)
    return jnp.einsum("bhtm,bmhd->bthd", p, v).reshape(B, S, XA_WIDTH)

def second_inputs(seed: int = 0) -> dict:
    key = jax.random.key(seed)
    ks = jax.random.split(key, 20)
    f32 = jnp.float32
    n_dn = (DEPTH + N_MIXERS - 1) // N_MIXERS
    n_sb = DEPTH // N_MIXERS

    def dense(k, shape, fan_in):
        return jax.random.normal(k, shape, f32) * fan_in ** -0.5

    def gain(k, shape):
        return 1.0 + 0.02 * jax.random.normal(k, shape, f32)

    dt = jnp.exp(jax.random.uniform(ks[10], (n_dn, DN_V_HEADS), f32,
                                    minval=math.log(1e-3), maxval=math.log(1e-1)))
    return {
        "x": jax.random.normal(ks[0], (BATCH, SEQ, D_MODEL), f32),
        "mem": jax.random.normal(ks[1], (BATCH, N_MEM, D_MODEL), f32),
        "norm_g": gain(ks[2], (DEPTH, D_MODEL)),
        "mem_norm_g": gain(ks[3], (D_MODEL,)),
        "mem_w_kv": dense(ks[4], (DEPTH, D_MODEL, 2 * XA_WIDTH), D_MODEL),
        "xa_q_norm_g": gain(ks[5], (DEPTH, XA_DIM)),
        "xa_k_norm_g": gain(ks[6], (DEPTH, XA_DIM)),
        "w_out": dense(ks[7], (DEPTH, INNER, D_MODEL), INNER),
        "dn_w_in": dense(ks[8], (n_dn, D_MODEL, DN_PROJ), D_MODEL),
        "dn_conv_w": dense(ks[9], (n_dn, DN_CONV, 2 * DN_QK_WIDTH + MIX_WIDTH), DN_CONV),
        "dn_a_log": jnp.log(jax.random.uniform(ks[11], (n_dn, DN_V_HEADS), f32, minval=1.0, maxval=16.0)),
        "dn_dt_bias": dt + jnp.log(-jnp.expm1(-dt)),
        "dn_out_norm_g": gain(ks[12], (n_dn, DN_HEAD_DIM)),
        "sb_w_in": dense(ks[13], (n_sb, D_MODEL, SB_PROJ), D_MODEL),
        "sb_q_norm_g": gain(ks[14], (n_sb, SB_HEAD_DIM)),
        "sb_k_norm_g": gain(ks[15], (n_sb, SB_HEAD_DIM)),
    }

def second_block(x, mem, norm_g, mem_norm_g, mem_w_kv, xa_q_norm_g, xa_k_norm_g, w_out,
              dn_w_in, dn_conv_w, dn_a_log, dn_dt_bias, dn_out_norm_g,
              sb_w_in, sb_q_norm_g, sb_k_norm_g):
    mem_n = rms_norm(mem, mem_norm_g)
    for i in range(DEPTH):
        h = rms_norm(x, norm_g[i])
        j = i // N_MIXERS
        if i % N_MIXERS == 0:
            proj = jnp.einsum("bsd,de->bse", h, dn_w_in[j])
            mix = deltanet_branch(proj[..., :DN_MIX_COLS], dn_conv_w[j], dn_a_log[j],
                                  dn_dt_bias[j], dn_out_norm_g[j])
        else:
            proj = jnp.einsum("bsd,de->bse", h, sb_w_in[j])
            mix = stick_breaking_branch(proj[..., :SB_MIX_COLS], sb_q_norm_g[j], sb_k_norm_g[j])
        xq = proj[..., -(XA_WIDTH + INNER):-INNER]
        z = proj[..., -INNER:]
        xa = memory_cross_attention(xq, mem_n, mem_w_kv[i], xa_q_norm_g[i], xa_k_norm_g[i])
        y = jnp.concatenate([mix, xa], axis=-1) * jax.nn.silu(z)
        x = x + jnp.einsum("bse,ed->bsd", y, w_out[i])
    return x


def setup_inputs(seed=0):
    out = dict(first_inputs(seed))
    for name, value in second_inputs(seed + 1).items():
        if name != "x":
            out[name + "_2"] = value
    return out


def reference(
    x, meta_tokens, norm1_g, w_in, w_alpha2, b_alpha, conv_w, conv_b, conv_ln_g, conv_ln_b,
    w_conv_out, gla_norm_g, w_gla_out, w_out, norm2_g, peer_wq, peer_k1, peer_k2, peer_u,
    peer_v, normf_g, mem_2, norm_g_2, mem_norm_g_2, mem_w_kv_2, xa_q_norm_g_2, xa_k_norm_g_2,
    w_out_2, dn_w_in_2, dn_conv_w_2, dn_a_log_2, dn_dt_bias_2, dn_out_norm_g_2, sb_w_in_2,
    sb_q_norm_g_2, sb_k_norm_g_2,
):
    x = first_block(
        x, meta_tokens, norm1_g, w_in, w_alpha2, b_alpha, conv_w, conv_b, conv_ln_g, conv_ln_b,
        w_conv_out, gla_norm_g, w_gla_out, w_out, norm2_g, peer_wq, peer_k1, peer_k2, peer_u,
        peer_v, normf_g,
    )
    return second_block(
        x, mem_2, norm_g_2, mem_norm_g_2, mem_w_kv_2, xa_q_norm_g_2, xa_k_norm_g_2, w_out_2,
        dn_w_in_2, dn_conv_w_2, dn_a_log_2, dn_dt_bias_2, dn_out_norm_g_2, sb_w_in_2,
        sb_q_norm_g_2, sb_k_norm_g_2,
    )


_drawn_inputs = setup_inputs


def setup_inputs(seed=0):
    import zlib

    import numpy as np

    out = dict(_drawn_inputs(seed))
    spreads = {}
    factors = {'conv_ln_g': 2.966,
     'conv_ln_b': 3.087,
     'gla_norm_g': 3.449,
     'norm_g_2': 3.802,
     'mem_norm_g_2': 8.0,
     'xa_q_norm_g_2': 8.0,
     'xa_k_norm_g_2': 8.0,
     'dn_out_norm_g_2': 6.136}
    for name, (base, spread) in spreads.items():
        noise = np.random.default_rng([zlib.crc32(name.encode()), seed]).standard_normal(out[name].shape)
        drawn = base * np.exp(spread * noise) if base else spread * noise
        out[name] = __import__('jax').numpy.asarray(drawn.astype(out[name].dtype))
    for name, factor in factors.items():
        out[name] = (out[name] * factor).astype(out[name].dtype)
    return out
```

```python
from contextlib import ExitStack, contextmanager

import concourse.bass as bass
from concourse import mybir

F32 = mybir.dt.float32
U32 = mybir.dt.uint32
ALU = mybir.AluOpType
ACT = mybir.ActivationFunctionType
AX = mybir.AxisListType
ds = bass.ds

P = 128
D = 2048
KT = D // P
TX = 256
NM = 16
T = NM + TX
MT = TX // P
EPS = 1e-6

PW = 256
RING = 4
TPP = PW // P
BANKS = 8
BANK = 512
TPI = RING * TPP

CONV_W = 31
GH, GDK, GDV, GRANK = 4, 256, 512, 16
C_Q = 2 * D
C_K = C_Q + GH * GDK
C_V = C_K + GH * GDK
C_R = C_V + GH * GDV
C_A = C_R + GH * GDV
C_MERGE = C_A + GRANK
QKT = GH * GDK // P
GC = 64
GTAU = 16.0
GSUB = 16
PH, NKEY, PTOP = 8, 128, 16
DH = 128
VH = 24
KH = 12
CQKV = 2 * KH * DH + VH * DH
C_AB = CQKV
C_XQ = CQKV + 2 * VH
XH, XD = 4, 256
C_Z = C_XQ + XH * XD
INNER = 2 * D
DCONV = 4

PAR = {}
_at = 0
for _name, _rows in (("norm1_g", 16), ("b_alpha", 8), ("conv_b", 16), ("conv_ln_g", 16), ("conv_ln_b", 16),
                     ("gla_norm_g", 16), ("norm2_g", 16)):
    PAR[_name] = (0, _at, _rows)
    _at += _rows
_at = 0
for _name, _rows in (("mem_norm_g_2", 16), ("norm_g_2", 16), ("xa_q_norm_g_2", 2), ("xa_k_norm_g_2", 2),
                     ("dn_out_norm_g_2", 1)):
    PAR[_name] = (1, _at, _rows)
    _at += _rows


def build(nc, a, out):
    outer = ExitStack()

    scopes = [[]]

    def sem(name):
        handle = nc.alloc_semaphore(name=name)
        scopes[-1].append(handle)
        return handle

    @contextmanager
    def phase():
        with ExitStack() as c:
            scopes.append([])
            yield c
            nc.clear_and_free_semaphores(scopes.pop())
            nc.all_engine_barrier()

    def sb(ctx, name, shape, dt=F32):
        return ctx.enter_context(nc.sbuf_tensor(name, shape, dt))

    with outer:
        PS = outer.enter_context(nc.psum_tensor("PS", [P, BANKS, BANK], F32))
        ring = sb(outer, "ring", [P, RING, KT, PW])
        ident = sb(outer, "ident", [P, P])
        ones = sb(outer, "ones", [P, P])
        eps_c = sb(outer, "eps_c", [P, 1])
        par = sb(outer, "par", [P, 2, P])
        cw = sb(outer, "cw", [P, CONV_W * KT])
        dcw = sb(outer, "dcw", [P, DCONV * CQKV // P])

        def pcol(name, k):
            t, at, _ = PAR[name]
            return par[:, t, at + k:at + k + 1]

        slot_loaded = [sem(f"slot_loaded{s}") for s in range(RING)]
        tile_ready = sem("tile_ready")

        def load_turn(sp, source, i, g0):
            for s in range(RING):
                sp.wait_ge(tile_ready, TPP * (g0 + s + 1) + i * TPI)
                sp.dma_start(ring[:, s, :, :], source(s, i)).then_inc(slot_loaded[s], 16)

        def load_panels(sp, source, turns, g0, first=1):
            if turns > first:
                with sp.Fori(first, turns) as i:
                    load_turn(sp, source, i, g0)

        def pe_tiles(pe, turns, g0, moving, width, taken, need, banks=BANKS):
            with pe.Fori(0, turns) as i:
                for s in range(RING):
                    pe.wait_ge(slot_loaded[s], 16 * (g0 // RING + 1) + i * 16)
                    for h in range(TPP):
                        t = s * TPP + h
                        pe.wait_ge(taken, need(i, t))
                        for k in range(KT):
                            last = nc.tensor.matmul(PS[:, t % banks, 0:width], ring[:, s, k, h * P:(h + 1) * P],
                                                    moving(k), start=(k == 0), stop=(k == KT - 1))
                        last.then_inc(tile_ready, 1)

        def ready_at(g0, i, t):
            return TPI + TPP * g0 + t + 1 + i * TPI

        def columns(w, at):
            wv = w.rearrange("(k p) n -> p k n", p=P)
            return lambda s, i: wv[:, :, ds(i * (RING * PW) + (at + s * PW), PW)]

        w_in = a["w_in"][0]
        w_in_v = w_in.rearrange("(k p) n -> p k n", p=P)

        def conv_panel(s, i):
            return w_in_v[:, :, ds(i * (2 * PW) + ((s % 2) * D + (s // 2) * PW), PW)]

        qkv_panel = columns(w_in, C_Q)
        r_panel = columns(w_in, C_R)
        merge_panel = columns(w_in, C_MERGE)
        convout_panel = columns(a["w_conv_out"][0], 0)
        glaout_panel = columns(a["w_gla_out"][0], 0)
        wout_panel = columns(a["w_out"][0], 0)
        wq_panel = columns(a["peer_wq"][0], 0)
        NCH = TX // GC
        RCH = KT // NCH
        r_dram = nc.dram_tensor("silu_r", (P, KT, TX), F32, kind="Internal").ap()

        one = outer.enter_context(ExitStack())
        conv_y = sb(one, "conv_y", [P, KT, TX])
        oT = sb(one, "oT", [P, KT, TX])
        xT = sb(one, "xT", [P, KT, T])
        gla = outer.enter_context(ExitStack())
        qkT = sb(gla, "qkT", [P, 2 * KT, T])
        vch = sb(gla, "vch", [P, KT, GC])
        wa2 = vch[0:GRANK, :, :].rearrange("p k n -> p (k n)")
        low = sb(gla, "low", [P, RCH * TX])
        alT = low[0:GRANK, 0:T]
        wal = low[:, T:T + KT * GRANK].rearrange("p (k n) -> p k n", n=GRANK)
        keep = low[:, T + KT * GRANK:2 * T + KT * GRANK]
        rbuf = low[:, :].rearrange("p (k n) -> p k n", n=TX)
        w_kv = a["mem_w_kv_2"][0]
        kvk_panel, kvv_panel = columns(w_kv, 0), columns(w_kv, XH * XD)
        w_dn = a["dn_w_in_2"][0]
        dqkv_panel, xq_panel, z_panel = columns(w_dn, 0), columns(w_dn, C_XQ), columns(w_dn, C_Z)
        w_out2_v = a["w_out_2"][0].rearrange("(f k p) n -> p f k n", p=P, f=2)

        def out2_panel(s, i):
            return w_out2_v[:, s % 2, :, ds(i * (2 * PW) + (s // 2) * PW, PW)]

        G_CONV, G_QKV, G_R, G_MG, G_CO, G_GO, G_WO, G_WQ = 0, 16, 32, 40, 56, 64, 72, 80
        G_KK, G_KV, G_DN, G_XQ, G_Z, G_O2 = 88, 92, 96, 120, 124, 140

        with phase() as c:
            xtok = qkT[:, :, :].rearrange("p k n -> p (k n)")[:, 0:(MT + 1) * D].rearrange("p (m n) -> p m n", n=D)
            o_flat = oT[:, :, :].rearrange("p k n -> p (k n)")
            sq = o_flat[:, 0:D]
            raw = o_flat[:, D:D + 8 * P].rearrange("p (t n) -> p t n", n=P)
            ss = sb(c, "ss", [P, 2, MT + 1])
            x_in, par_in, id_done, sq_done, rt_done, rs_done, xs_done, tr, ev_act, ev_dve, wal_in = (
                sem(n) for n in ("x_in", "par_in", "id_done", "sq_done", "rt_done", "rs_done", "xs_done",
                                 "xt_transposed", "xt_odd_out", "xt_even_out", "wal_in"))
            n_par = [0]
            with nc.Block() as block:
                @block.sync
                def _(sp):
                    for m in range(MT):
                        sp.dma_start(xtok[:, m, :], a["x"][0, m * P:(m + 1) * P, :]).then_inc(x_in, 16)
                    sp.dma_start(xtok[0:NM, MT, :], a["meta_tokens"]).then_inc(x_in, 16)
                    sp.wait_ge(id_done, 3)
                    for name, (t, at, rows) in PAR.items():
                        v = a[name]
                        v = v[0] if len(v.shape) == 2 else v
                        sp.dma_start(raw[at:at + rows, t, :], v.rearrange("(k p) -> k p", p=P)).then_inc(par_in, 16)
                        n_par[0] += 16
                    taps = a["conv_w"][0].rearrange("w (k p) -> (w k) p", p=P)
                    for n in range(4):
                        sp.dma_start(raw[0:124, 2 + n, :], taps[124 * n:124 * (n + 1), :]).then_inc(par_in, 16)
                    dtaps = a["dn_conv_w_2"][0].rearrange("w (k p) -> (w k) p", p=P)
                    for n in range(2):
                        sp.dma_start(raw[0:96, 6 + n, :], dtaps[96 * n:96 * (n + 1), :]).then_inc(par_in, 16)
                    n_par[0] += 96
                    sp.dma_start(wal[:, :, :], w_in_v[:, :, C_A:C_MERGE]).then_inc(wal_in, 16)
                    sp.dma_start(wa2, a["w_alpha2"][0]).then_inc(wal_in, 16)
                    load_turn(sp, conv_panel, 0, G_CONV)
                    sp.wait_ge(wal_in, 32)

                @block.gpsimd
                def _(pool):
                    nc.gpsimd.memset(ones[:, :], 1.0).then_inc(id_done, 1)
                    nc.gpsimd.memset(eps_c[:, :], EPS).then_inc(id_done, 1)
                    nc.gpsimd.memset(raw[:, :, :], 0.0).then_inc(id_done, 1)
                    pool.wait_ge(id_done, 3)
                    nc.gpsimd.affine_select(out=ident[:, :], in_=ones[:, :], compare_op=ALU.is_equal, fill=0.0,
                                            base=0, pattern=[[-1, P]], channel_multiplier=1).then_inc(id_done, 1)

                @block.scalar
                def _(act):
                    act.wait_ge(x_in, 48)
                    for m, rows in enumerate((P, P, NM)):
                        if m:
                            act.wait_ge(sq_done, m)
                        nc.scalar.activation(sq[0:rows, 0:D], xtok[0:rows, m, :], ACT.Square,
                                             accum_out=ss[0:rows, 0, m:m + 1]).then_inc(sq_done, 1)
                    act.wait_ge(sq_done, 3)
                    act.wait_ge(id_done, 4)
                    for m, rows in enumerate((P, P, NM)):
                        nc.scalar.activation(ss[0:rows, 1, m:m + 1], ss[0:rows, 0, m:m + 1], ACT.Sqrt,
                                             bias=eps_c[0:rows, :], scale=1.0 / D).then_inc(rt_done, 1)
                    for k in range(1, KT, 2):
                        act.wait_ge(tr, k + 2)
                        nc.scalar.activation(xT[:, k, :], PS[:, k % BANKS, 0:T], ACT.Copy,
                                             scale=pcol("norm1_g", k)).then_inc(ev_act, 1)

                @block.vector
                def _(dve):
                    dve.wait_ge(rt_done, 3)
                    for m, rows in enumerate((P, P, NM)):
                        nc.vector.reciprocal(ss[0:rows, 0, m:m + 1], ss[0:rows, 1, m:m + 1]).then_inc(rs_done, 1)
                    dve.wait_ge(rs_done, 3)
                    for m, rows in enumerate((P, P, NM)):
                        nc.vector.tensor_scalar(xtok[0:rows, m, :], xtok[0:rows, m, :], ss[0:rows, 0, m:m + 1],
                                                None, ALU.mult).then_inc(xs_done, 1)
                    dve.wait_ge(tr, 1)
                    nc.vector.tensor_copy(par[:, :, :], PS[:, 6, 0:2 * P].rearrange("p (t n) -> p t n", t=2)).then_inc(xs_done, 1)
                    nc.vector.tensor_copy(cw[:, :], PS[:, 7, 0:CONV_W * KT]).then_inc(xs_done, 1)
                    nc.vector.tensor_copy(dcw[:, :], PS[:, 5, 0:192]).then_inc(xs_done, 1)
                    dve.wait_ge(xs_done, 6)
                    for k in range(0, KT, 2):
                        dve.wait_ge(tr, k + 2)
                        nc.vector.tensor_scalar(xT[:, k, :], PS[:, k % BANKS, 0:T], pcol("norm1_g", k),
                                                None, ALU.mult).then_inc(ev_dve, 1)

                @block.tensor
                def _(pe):
                    pe.sem_inc(tile_ready, TPI)
                    pe.wait_ge(par_in, n_par[0])
                    pe.wait_ge(id_done, 4)
                    for t in range(2):
                        nc.tensor.transpose(PS[:, 6, t * P:(t + 1) * P], raw[:, t, :], ident[:, :])
                    for n in range(4):
                        nc.tensor.transpose(PS[:, 7, n * 124:(n + 1) * 124], raw[0:124, 2 + n, :], ident[0:124, 0:124])
                    for n in range(2):
                        last = nc.tensor.transpose(PS[:, 5, n * 96:(n + 1) * 96], raw[0:96, 6 + n, :], ident[0:96, 0:96])
                    last.then_inc(tr, 1)
                    pe.wait_ge(xs_done, 6)
                    for k in range(KT):
                        if k >= BANKS:
                            pe.wait_ge(ev_act if k % 2 else ev_dve, (k - BANKS) // 2 + 1)
                        b = PS[:, k % BANKS, :]
                        nc.tensor.transpose(b[:, 0:NM], xtok[0:NM, MT, k * P:(k + 1) * P], ident[0:NM, 0:NM])
                        for m in range(MT):
                            last = nc.tensor.transpose(b[:, NM + m * P:NM + (m + 1) * P],
                                                       xtok[:, m, k * P:(k + 1) * P], ident[:, :])
                        last.then_inc(tr, 1)

        with phase() as c:
            gate = sb(c, "gate", [P, 4, T])
            PADL = CONV_W - 1 - NM
            hp = sb(c, "hp", [P, 4, PADL + T])
            acc = sb(c, "acc", [P, 4, TX])
            gate_ready, glu_taken, dchain, qkv_taken, al_ready, pad_done = (
                sem(n) for n in ("gate_ready", "glu_taken", "conv_chain", "qkv_taken",
                                 "alow_ready", "pad_done"))
            with nc.Block() as block:
                @block.sync
                def _(sp):
                    load_panels(sp, conv_panel, 4, G_CONV)
                    load_panels(sp, qkv_panel, 4, G_QKV, 0)
                    load_turn(sp, r_panel, 0, G_R)

                @block.tensor
                def _(pe):
                    pe_tiles(pe, 4, G_CONV, lambda k: xT[:, k, :], T, glu_taken,
                             lambda i, t: i * 4 + (2 * (t // 4) + t % 2 + 1))
                    pe.wait_ge(glu_taken, 4 + 16)
                    pe_tiles(pe, 4, G_QKV, lambda k: xT[:, k, :], T, qkv_taken, lambda i, t: i * TPI + (t + 1))
                    pe.wait_ge(qkv_taken, 8 + 32)
                    for k in range(KT):
                        last = nc.tensor.matmul(PS[0:GRANK, 0, 0:T], wal[:, k, :], xT[:, k, :],
                                                start=(k == 0), stop=(k == KT - 1))
                    last.then_inc(al_ready, 1)

                @block.scalar
                def _(act):
                    act.sem_inc(qkv_taken, 8)
                    with act.Fori(0, 4) as i:
                        for slot in range(4):
                            t = 4 * (slot // 2) + 2 + slot % 2
                            act.wait_ge(tile_ready, ready_at(G_CONV, i, t))
                            act.wait_ge(glu_taken, i * 4 + slot + 1)
                            nc.scalar.activation(gate[:, slot, :], PS[:, t, 0:T], ACT.Sigmoid).then_inc(gate_ready, 1)
                    with act.Fori(0, 4) as i:
                        for t in range(TPI):
                            act.wait_ge(tile_ready, ready_at(G_QKV, i, t))
                            nc.scalar.activation(qkT[:, ds(i * TPI + t, 1), :], PS[:, t, 0:T], ACT.Copy).then_inc(qkv_taken, 1)
                    act.wait_ge(al_ready, 1)
                    nc.scalar.activation(alT[:, :], PS[0:GRANK, 0, 0:T], ACT.Copy)

                @block.vector
                def _(dve):
                    nc.vector.memset(hp[:, :, 0:PADL], 0.0).then_inc(pad_done, 1)
                    dve.wait_ge(pad_done, 1)
                    dve.sem_inc(glu_taken, 4)
                    per = 4 * CONV_W
                    with dve.Fori(0, 4) as i:
                        n = 0
                        for pr in range(2):
                            for h in range(2):
                                slot = 2 * pr + h
                                dve.wait_ge(gate_ready, i * 4 + (slot + 1))
                                dve.wait_ge(dchain, i * per + n)
                                nc.vector.tensor_tensor(hp[:, slot, PADL:PADL + T], PS[:, 4 * pr + h, 0:T],
                                                        gate[:, slot, :], ALU.mult).then_inc(glu_taken, 1)
                            dve.wait_ge(glu_taken, i * 4 + (4 + 2 * pr + 2))
                            for j in range(CONV_W):
                                for h in range(2):
                                    slot = 2 * pr + h
                                    w = cw[:, ds(i * 4 + (j * KT + slot), 1)]
                                    src = hp[:, slot, j:j + TX]
                                    if j == 0:
                                        t_, at, _ = PAR["conv_b"]
                                        ins = nc.vector.tensor_scalar(acc[:, slot, :], src, w,
                                                                      par[:, t_, ds(i * 4 + (at + slot), 1)],
                                                                      ALU.mult, ALU.add)
                                    else:
                                        dve.wait_ge(dchain, i * per + (n - 1))
                                        dst = acc[:, slot, :] if j < CONV_W - 1 else conv_y[:, ds(i * 4 + slot, 1), :]
                                        ins = nc.vector.scalar_tensor_tensor(dst, src, w, acc[:, slot, :],
                                                                             ALU.mult, ALU.add)
                                    ins.then_inc(dchain, 1)
                                    n += 1
                        assert n == per

        with phase() as c:
            NT = 2 * GH
            bT = sb(c, "bT", [P, NT, T])
            ks = sb(c, "ks", [P, NT, GC // GSUB, GC])
            lsf = ks[:, :, :, :].rearrange("p t s n -> p (t s n)")
            S = sb(c, "S", [P, NT, GDV])
            S_flat = S[:, :, :].rearrange("p t n -> p (t n)")
            ls = S_flat[:, 0:NT * T].rearrange("p (t n) -> p t n", n=T)
            qs = sb(c, "qs", [P, NT, GC])
            qe = sb(c, "qe", [P, NT, GC])
            kd = sb(c, "kd", [P, NT, GC])
            ref = sb(c, "ref", [P, NT, GC // GSUB])
            dec = sb(c, "dec", [P, NT, 1])
            caus = sb(c, "caus", [GC, GC])
            attS = sb(c, "attS", [GC, GH, GC])
            kdt = vch[0:GC, :, :].rearrange("p k n -> p (k n)").rearrange("p (t n) -> p t n", n=P)
            vt = sb(c, "vt", [GC, GH, GDV])
            (cst, z_ready, z_out, lg, zchain, diff_ready, exp_ready, mul_ready, v_ready, kt_done, kt_out, vtr_done,
             pe_step, vt_out, att_done, att_out, o_done, o_out, s_done, s_out) = (sem(n) for n in (
                "gla_consts", "z_ready", "z_out", "lg", "z_chain", "diff_ready", "exp_ready", "mul_ready", "v_ready",
                "kd_transposed", "kdt_out", "v_transposed", "pe_step", "vt_out", "att_done", "att_out", "o_done", "o_out",
                "state_done", "state_out"))
            r_taken, r_stored = sem("r_taken"), sem("r_stored")
            NSUB = GC // GSUB
            q_, k_, v_ = (lambda t0, n: qkT[:, 0:NT, ds(t0, n)], lambda t0, n: qkT[:, NT:2 * NT, ds(t0, n)],
                          lambda t0, n: qkT[:, 2 * NT:, ds(t0, n)])

            with nc.Block() as block:
                @block.sync
                def _(sp):
                    load_panels(sp, r_panel, 2, G_R)
                    load_turn(sp, merge_panel, 0, G_MG)

                @block.gpsimd
                def _(pool):
                    nc.gpsimd.memset(keep[:, :], 1.0).then_inc(cst, 1)
                    pool.wait_ge(cst, 1)
                    nc.gpsimd.memset(keep[:, 0:1], 0.0).then_inc(cst, 1)
                    nc.gpsimd.memset(keep[:, NM:T].rearrange("p (c n) -> p c n", n=GC)[:, :, 0:1], 0.0).then_inc(cst, 1)
                    nc.gpsimd.affine_select(out=caus[:, :], in_=ones[0:GC, 0:GC], compare_op=ALU.is_ge, fill=0.0,
                                            base=0, pattern=[[1, GC]], channel_multiplier=-1).then_inc(cst, 1)
                    pool.wait_ge(z_ready, NT)
                    nc.gpsimd.tensor_copy(vch[:, :, 0:NM], v_(0, NM)).then_inc(v_ready, 1)
                    with pool.Fori(0, NCH) as i:
                        pool.wait_ge(s_done, i * NT + NT)
                        nc.gpsimd.tensor_copy(vch[:, :, :], v_(i * GC + NM, GC)).then_inc(v_ready, 1)
                        pool.wait_ge(r_taken, i + 1)
                        nc.gpsimd.dma_start(r_dram[:, ds(i * RCH, RCH), :], rbuf[:, :, :]).then_inc(r_stored, 16)

                @block.tensor
                def _(pe):
                    for t in range(NT):
                        nc.tensor.matmul(PS[:, t, 0:T], wa2[:, t * P:(t + 1) * P], alT[:, :], start=True,
                                         stop=True).then_inc(z_ready, 1)
                    pe.wait_ge(z_out, NT)

                    def v_transposes(n, L):
                        pe.wait_ge(v_ready, n + 1)
                        pe.wait_ge(s_out, n * NT)
                        pe.sem_inc(pe_step, 1)
                        for e in range(KT):
                            last = nc.tensor.transpose(PS[0:L, 1 + e // 4, (e % 4) * P:(e % 4 + 1) * P],
                                                       vch[:, e, 0:L], ident[:, :])
                        last.then_inc(vtr_done, 1)

                    def k_transposes(n, L, muls):
                        pe.wait_ge(mul_ready, muls)
                        for t in range(NT):
                            if t % 4 == 0:
                                pe.wait_ge(kt_out, n * 2 + t // 4)
                                pe.sem_inc(pe_step, 1)
                            last = nc.tensor.transpose(PS[0:L, 7, (t % 4) * P:(t % 4 + 1) * P],
                                                       kd[:, t, 0:L], ident[:, :])
                            if t % 4 == 3:
                                last.then_inc(kt_done, 1)

                    def state_products(n, L):
                        pe.wait_ge(vt_out, n * 2 + 2)
                        pe.wait_ge(kt_out, n * 2 + 2)
                        for t in range(NT):
                            if t >= 4:
                                pe.wait_ge(s_out, n * NT + (t - 3))
                            nc.tensor.matmul(PS[:, 1 + t % 4, :], kdt[0:L, t, :], vt[0:L, t // 2, :], start=True,
                                             stop=True).then_inc(s_done, 1)

                    v_transposes(0, NM)
                    k_transposes(0, NM, 1)
                    state_products(0, NM)

                    def r_products(j, c2, q0, q1):
                        for q in range(q0, q1):
                            s, t = 2 * c2 + q // TPP, c2 * RCH + q
                            if q % TPP == 0:
                                pe.wait_ge(slot_loaded[s], 16 * (G_R // RING + 1) + j * 16)
                            for k in range(KT):
                                last = nc.tensor.matmul(PS[:, 5 + q // 2, (q % 2) * TX:(q % 2 + 1) * TX],
                                                        ring[:, s, k, (t % TPP) * P:(t % TPP + 1) * P], xT[:, k, NM:T],
                                                        start=(k == 0), stop=(k == KT - 1))
                            last.then_inc(tile_ready, 1)

                    def chunk(i, j, c2):
                        pe.wait_ge(o_out, i + 1)
                        r_products(j, c2, 0, 2)
                        v_transposes(i + 1, GC)
                        r_products(j, c2, 2, 3)
                        k_transposes(i + 1, GC, i * 7 + 8)
                        for h in range(GH):
                            for sub in range(NSUB):
                                for d in range(2):
                                    last = nc.tensor.matmul(
                                        PS[0:GC, 0, h * GC + sub * GSUB:h * GC + (sub + 1) * GSUB],
                                        ks[:, 2 * h + d, sub, :], qs[:, 2 * h + d, sub * GSUB:(sub + 1) * GSUB],
                                        start=(d == 0), stop=(d == 1))
                        last.then_inc(att_done, 1)
                        r_products(j, c2, 3, 4)
                        pe.wait_ge(vt_out, i * 2 + 4)
                        pe.wait_ge(att_out, i + 1)
                        pe.wait_ge(r_taken, i + 1)
                        for e in range(KT):
                            h, b = e // 4, PS[:, 5 + e // 8, (e % 8) * GC:(e % 8 + 1) * GC]
                            for d in range(2):
                                nc.tensor.matmul(b, S[:, 2 * h + d, (e % 4) * P:(e % 4 + 1) * P],
                                                 qe[:, 2 * h + d, :], start=(d == 0), stop=False)
                            last = nc.tensor.matmul(b, vt[:, h, (e % 4) * P:(e % 4 + 1) * P], attS[:, h, :],
                                                    start=False, stop=True)
                        last.then_inc(o_done, 1)
                        state_products(i + 1, GC)

                    with pe.Fori(0, NCH // 2) as j:
                        for c2 in range(2):
                            chunk(j * 2 + c2, j, c2)

                @block.scalar
                def _(act):
                    tb, at, _ = PAR["b_alpha"]
                    for t in range(NT):
                        act.wait_ge(z_ready, t + 1)
                        nc.scalar.activation(bT[:, t, :], PS[:, t, 0:T], ACT.Identity,
                                             bias=par[:, tb, at + t:at + t + 1]).then_inc(z_out, 1)
                    act.wait_ge(z_out, NT)
                    nc.scalar.activation(ls, bT[:, :, :], ACT.Abs).then_inc(lg, 1)
                    act.wait_ge(lg, 1)
                    nc.scalar.activation(ls, ls, ACT.Exp, scale=-1.0).then_inc(lg, 1)
                    act.wait_ge(lg, 2)
                    nc.scalar.activation(ls, ls, ACT.Ln, bias=1.0).then_inc(lg, 1)
                    EXPK = dict(func=ACT.Exp, scale=1.0 / GTAU)

                    def token_major(n, L):
                        act.wait_ge(vtr_done, n + 1)
                        for half in range(2):
                            nc.scalar.activation(vt[0:L, 2 * half:2 * half + 2, :], PS[0:L, 1 + 2 * half:3 + 2 * half, :],
                                                 ACT.Copy).then_inc(vt_out, 1)
                        for half in range(2):
                            act.wait_ge(kt_done, n * 2 + (half + 1))
                            nc.scalar.activation(kdt[0:L, 4 * half:4 * half + 4, :],
                                                 PS[0:L, 7, :].rearrange("p (t n) -> p t n", n=P), ACT.Copy).then_inc(kt_out, 1)

                    act.wait_ge(diff_ready, 1)
                    nc.scalar.activation(kd[:, :, 0:NM], kd[:, :, 0:NM], **EXPK).then_inc(exp_ready, 1)
                    token_major(0, NM)
                    act.sem_inc(o_out, 1)
                    with act.Fori(0, NCH) as i:
                        act.wait_ge(diff_ready, i * 9 + 10)
                        nc.scalar.activation(kd[:, :, :], kd[:, :, :], **EXPK).then_inc(exp_ready, 1)
                        nc.scalar.activation(qe[:, :, :], bT[:, :, ds(i * GC + NM, GC)], **EXPK).then_inc(exp_ready, 1)
                        nc.scalar.activation(dec[:, :, :], bT[:, :, ds(i * GC + (NM + GC - 1), 1)], **EXPK).then_inc(exp_ready, 1)
                        nc.scalar.activation(qs[:, :, :], qs[:, :, :], **EXPK).then_inc(exp_ready, 1)
                        for sub in range(NSUB):
                            w = (sub + 1) * GSUB
                            nc.scalar.activation(ks[:, :, sub, 0:w], ks[:, :, sub, 0:w], **EXPK).then_inc(exp_ready, 1)
                        token_major(i + 1, GC)
                        act.wait_ge(tile_ready, i * RCH + (TPI + TPP * G_R + RCH))
                        nc.scalar.activation(rbuf[:, :, :], PS[:, 5:7, :].rearrange("p b (t n) -> p (b t) n", n=TX),
                                             ACT.Silu).then_inc(r_taken, 1)
                        act.wait_ge(r_stored, i * 16 + 16)
                        act.wait_ge(o_done, i + 1)
                        nc.scalar.activation(oT[:, :, ds(i * GC, GC)],
                                             PS[:, 5:7, :].rearrange("p b (e n) -> p (b e) n", n=GC),
                                             ACT.Copy).then_inc(o_out, 1)

                @block.vector
                def _(dve):
                    dve.wait_ge(lg, 3)
                    dve.wait_ge(cst, 4)
                    nc.vector.scalar_tensor_tensor(bT[:, :, :], bT[:, :, :], 0.0, ls, ALU.min, ALU.subtract).then_inc(zchain, 1)
                    nc.vector.memset(lsf, 0.0).then_inc(zchain, 1)
                    dve.wait_ge(zchain, 1)
                    for t in range(NT):
                        nc.vector.tensor_tensor_scan(bT[:, t, :], keep[:, :], bT[:, t, :], 0.0, ALU.mult,
                                                     ALU.add).then_inc(zchain, 1)
                    nc.vector.memset(ref[:, :, 0:1], 0.0).then_inc(zchain, 1)
                    Z0 = 2 + NT + 1
                    dve.wait_ge(zchain, Z0)
                    nc.vector.tensor_tensor(kd[:, :, 0:NM], bT[:, :, NM - 1:NM].broadcast_to([P, NT, NM]),
                                            bT[:, :, 0:NM], ALU.subtract).then_inc(diff_ready, 1)
                    dve.wait_ge(exp_ready, 1)
                    nc.vector.tensor_tensor(kd[:, :, 0:NM], kd[:, :, 0:NM], k_(0, NM), ALU.mult).then_inc(mul_ready, 1)
                    for t in range(NT):
                        dve.wait_ge(s_done, t + 1)
                        nc.vector.tensor_copy(S[:, t, :], PS[:, 1 + t % 4, :]).then_inc(s_out, 1)
                    with dve.Fori(0, NCH) as i:
                        def b(at, w):
                            return bT[:, :, ds(i * GC + (NM + at), w)]
                        dve.wait_ge(s_done, i * NT + NT)
                        dve.wait_ge(s_out, i * NT + NT)
                        for sub in range(1, NSUB):
                            nc.vector.tensor_copy(ref[:, :, sub:sub + 1], b(sub * GSUB - 1, 1)).then_inc(zchain, 1)
                        nc.vector.tensor_tensor(kd[:, :, :], b(GC - 1, 1).broadcast_to([P, NT, GC]), b(0, GC),
                                                ALU.subtract).then_inc(diff_ready, 1)
                        dve.wait_ge(zchain, i * (NSUB - 1) + (Z0 + NSUB - 1))
                        for sub in range(NSUB):
                            w = (sub + 1) * GSUB
                            nc.vector.tensor_tensor(ks[:, :, sub, 0:w], ref[:, :, sub:sub + 1].broadcast_to([P, NT, w]),
                                                    b(0, w), ALU.subtract).then_inc(diff_ready, 1)
                            nc.vector.tensor_tensor(qs[:, :, sub * GSUB:w], b(sub * GSUB, GSUB),
                                                    ref[:, :, sub:sub + 1].broadcast_to([P, NT, GSUB]),
                                                    ALU.subtract).then_inc(diff_ready, 1)
                        dve.wait_ge(exp_ready, i * 8 + 9)
                        kc, qc = k_(i * GC + NM, GC), q_(i * GC + NM, GC)
                        nc.vector.tensor_tensor(kd[:, :, :], kd[:, :, :], kc, ALU.mult).then_inc(mul_ready, 1)
                        for qx in (qs, qe):
                            nc.vector.scalar_tensor_tensor(qx[:, :, :], qx[:, :, :], GDK ** -0.5, qc, ALU.mult,
                                                           ALU.mult).then_inc(mul_ready, 1)
                        for sub in range(NSUB):
                            w = (sub + 1) * GSUB
                            nc.vector.tensor_tensor(ks[:, :, sub, 0:w], ks[:, :, sub, 0:w], k_(i * GC + NM, w),
                                                    ALU.mult).then_inc(mul_ready, 1)
                        dve.wait_ge(att_done, i + 1)
                        nc.vector.tensor_tensor(attS[:, :, :], PS[0:GC, 0, 0:GH * GC].rearrange("p (h n) -> p h n", n=GC),
                                                caus[:, :].unsqueeze(1).broadcast_to([GC, GH, GC]),
                                                ALU.mult).then_inc(att_out, 1)
                        for t in range(NT):
                            dve.wait_ge(s_done, i * NT + (NT + t + 1))
                            nc.vector.scalar_tensor_tensor(S[:, t, :], S[:, t, :], dec[:, t, :], PS[:, 1 + t % 4, :],
                                                           ALU.mult, ALU.add).then_inc(s_out, 1)
        gla.close()

        mix = outer.enter_context(ExitStack())
        mixT = sb(mix, "mixT", [P, KT, TX])
        with phase() as c:
            rT = sb(c, "rT", [P, KT, TX])
            mgT = sb(c, "mgT", [P, 2 * KT, TX])
            sqb = sb(c, "sqb", [P, KT, TX])
            stat = sb(c, "stat", [P, 1 + GH, TX])
            mu, rso = stat[:, 0, :], stat[:, 1:, :]
            prod = sb(c, "prod", [P, 4, TX])
            (sq_ready, sums, r_in, mg_taken, centred, rt_ready, cchain, y_ready, g_ready, co_taken, go_taken,
             pr_ready) = (sem(n) for n in (
                "squares_ready", "sums_ready", "r_in", "merge_taken", "centred", "roots_ready", "norm_chain",
                "conv_branch_ready", "gla_branch_ready", "conv_out_taken", "gla_out_taken", "product_ready"))
            with nc.Block() as block:
                @block.sync
                def _(sp):
                    sp.dma_start(rT[:, :, :], r_dram).then_inc(r_in, 16)
                    load_panels(sp, merge_panel, 4, G_MG)
                    load_panels(sp, convout_panel, 2, G_CO, 0)
                    load_panels(sp, glaout_panel, 2, G_GO, 0)
                    load_turn(sp, wout_panel, 0, G_WO)

                @block.tensor
                def _(pe):
                    for k in range(KT):
                        last = nc.tensor.matmul(PS[:, 4, 0:TX], ones[:, :], conv_y[:, k, :], start=(k == 0),
                                                stop=(k == KT - 1))
                    last.then_inc(sums, 1)
                    pe.wait_ge(sq_ready, 1)
                    for h in range(GH):
                        for e in range(GDV // P):
                            last = nc.tensor.matmul(PS[:, 5 + h // 2, (h % 2) * TX:(h % 2 + 1) * TX], ones[:, :],
                                                    mixT[:, h * (GDV // P) + e, :], start=(e == 0), stop=(e == 3))
                    last.then_inc(sums, 1)
                    pe_tiles(pe, 2, G_MG, lambda k: xT[:, k, NM:T], TX, mg_taken, lambda i, t: i * TPI + (t + 1), 4)
                    pe.wait_ge(sq_ready, 2)
                    for k in range(KT):
                        last = nc.tensor.matmul(PS[:, 7, 0:TX], ones[:, :], sqb[:, k, :], start=(k == 0),
                                                stop=(k == KT - 1))
                    last.then_inc(sums, 1)
                    pe_tiles(pe, 2, G_MG + 2 * RING, lambda k: xT[:, k, NM:T], TX, mg_taken,
                             lambda i, t: i * TPI + (2 * TPI + t + 1), 4)
                    pe.wait_ge(mg_taken, 4 + 4 * TPI)
                    pe.wait_ge(y_ready, KT)
                    pe_tiles(pe, 2, G_CO, lambda k: conv_y[:, k, :], TX, co_taken, lambda i, t: i * TPI + (t + 1), 4)
                    pe.wait_ge(co_taken, 4 + 2 * TPI)
                    pe.wait_ge(g_ready, GH + KT)
                    pe_tiles(pe, 2, G_GO, lambda k: oT[:, k, :], TX, go_taken, lambda i, t: i * TPI + (t + 1), 4)

                @block.scalar
                def _(act):
                    act.sem_inc(mg_taken, 4)
                    nc.scalar.activation(mixT[:, :, :], oT[:, :, :], ACT.Square).then_inc(sq_ready, 1)
                    act.wait_ge(centred, 2)
                    nc.scalar.activation(sqb[:, :, :], conv_y[:, :, :], ACT.Square).then_inc(sq_ready, 1)
                    act.wait_ge(sums, 2)
                    nc.scalar.activation(rso, PS[:, 5:7, :].rearrange("p b (h n) -> p (b h) n", n=TX), ACT.Sqrt,
                                         bias=eps_c[:, :], scale=1.0 / GDV).then_inc(rt_ready, 1)

                    def merge_gates(i0, i1):
                        with act.Fori(i0, i1) as i:
                            for t in range(TPI):
                                act.wait_ge(tile_ready, ready_at(G_MG, i, t))
                                nc.scalar.activation(mgT[:, ds(i * TPI + t, 1), :], PS[:, t % 4, 0:TX],
                                                     ACT.Sigmoid).then_inc(mg_taken, 1)
                    merge_gates(0, 2)
                    act.wait_ge(sums, 3)
                    act.wait_ge(centred, 3)
                    nc.scalar.activation(mu, PS[:, 7, 0:TX], ACT.Sqrt, bias=eps_c[:, :], scale=1.0 / D).then_inc(rt_ready, 1)
                    merge_gates(2, 4)
                    act.wait_ge(cchain, 3)
                    for k in range(KT):
                        nc.scalar.activation(conv_y[:, k, :], conv_y[:, k, :], ACT.Silu, bias=pcol("conv_ln_b", k),
                                             scale=pcol("conv_ln_g", k)).then_inc(y_ready, 1)

                @block.vector
                def _(dve):
                    dve.sem_inc(co_taken, 4)
                    dve.sem_inc(go_taken, 4)
                    dve.sem_inc(pr_ready, 1)
                    dve.wait_ge(sums, 1)
                    nc.vector.tensor_scalar(mu, PS[:, 4, 0:TX], 1.0 / D, None, ALU.mult).then_inc(centred, 1)
                    dve.wait_ge(centred, 1)
                    nc.vector.tensor_tensor(conv_y[:, :, :], conv_y[:, :, :], mu.unsqueeze(1).broadcast_to([P, KT, TX]),
                                            ALU.subtract).then_inc(centred, 1)
                    dve.wait_ge(centred, 2)
                    dve.sem_inc(centred, 1)
                    dve.wait_ge(rt_ready, 1)
                    nc.vector.reciprocal(rso, rso).then_inc(cchain, 1)
                    dve.wait_ge(cchain, 1)
                    for h in range(GH):
                        n = GDV // P
                        nc.vector.tensor_tensor(oT[:, h * n:(h + 1) * n, :], oT[:, h * n:(h + 1) * n, :],
                                                rso[:, h:h + 1, :].broadcast_to([P, n, TX]), ALU.mult).then_inc(g_ready, 1)
                    dve.wait_ge(rt_ready, 2)
                    nc.vector.reciprocal(mu, mu).then_inc(cchain, 1)
                    dve.wait_ge(cchain, 2)
                    nc.vector.tensor_tensor(conv_y[:, :, :], conv_y[:, :, :], mu.unsqueeze(1).broadcast_to([P, KT, TX]),
                                            ALU.mult).then_inc(cchain, 1)
                    dve.wait_ge(g_ready, GH)
                    dve.wait_ge(r_in, 16)
                    for k in range(KT):
                        nc.vector.scalar_tensor_tensor(oT[:, k, :], oT[:, k, :], pcol("gla_norm_g", k), rT[:, k, :],
                                                       ALU.mult, ALU.mult).then_inc(g_ready, 1)
                    dve.wait_ge(mg_taken, 4 + 4 * TPI)
                    with dve.Fori(0, 2) as i:
                        for t in range(TPI):
                            dve.wait_ge(tile_ready, ready_at(G_CO, i, t))
                            nc.vector.tensor_tensor(mixT[:, ds(i * TPI + t, 1), :], PS[:, t % 4, 0:TX],
                                                    mgT[:, ds(i * TPI + t, 1), :], ALU.mult).then_inc(co_taken, 1)
                    dve.wait_ge(co_taken, 4 + 2 * TPI)
                    with dve.Fori(0, 2) as i:
                        for t in range(TPI):
                            dve.wait_ge(tile_ready, ready_at(G_GO, i, t))
                            dve.wait_ge(pr_ready, i * TPI + (1 + max(t - 3, 0)))
                            nc.vector.tensor_tensor(prod[:, t % 4, :], PS[:, t % 4, 0:TX],
                                                    mgT[:, ds(i * TPI + (KT + t), 1), :], ALU.mult).then_inc(go_taken, 1)
                            dve.wait_ge(go_taken, i * TPI + (4 + t + 1))
                            nc.vector.tensor_tensor(mixT[:, ds(i * TPI + t, 1), :], mixT[:, ds(i * TPI + t, 1), :],
                                                    prod[:, t % 4, :], ALU.add).then_inc(pr_ready, 1)

        def flat(t):
            return t[:, :, :].rearrange("p k n -> p (k n)")

        h_tok = flat(conv_y).rearrange("p (m n) -> p m n", n=D)
        xn_tok = flat(oT).rearrange("p (m n) -> p m n", n=D)
        xnT = flat(xT)[:, 0:KT * TX].rearrange("p (k n) -> p k n", n=TX)
        scores = flat(xT)[:, 0:2 * PH * 2 * NKEY].rearrange("p (h n) -> p h n", n=2 * NKEY)
        q2T = mixT

        def pe_token_tiles(pe, turns, g0, stationary, taken, need, banks=BANKS):
            with pe.Fori(0, turns) as i:
                for s in range(RING):
                    pe.wait_ge(slot_loaded[s], 16 * (g0 // RING + 1) + i * 16)
                    for m in range(MT):
                        t = s * MT + m
                        pe.wait_ge(taken, need(i, t))
                        for k in range(KT):
                            last = nc.tensor.matmul(PS[:, t % banks, 0:PW], stationary(k, m), ring[:, s, k, :],
                                                    start=(k == 0), stop=(k == KT - 1))
                        last.then_inc(tile_ready, 1)

        with phase() as c:
            kraw = sb(c, "kraw", [P, 2 * PH, P])
            kT = sb(c, "kT", [P, 2 * PH, P])
            grow = sb(c, "grow", [P, D])
            ssq = sb(c, "ssq", [P, D])
            rs2 = sb(c, "rs2", [P, 2, MT])
            (h_in, g_in, k_in, wo_taken, wq_taken, sq_done, rt_done, rs_done, xn_done, tr_done, tr_act, tr_dve, kt_tr,
             kt_out, sc_done, sc_act, sc_dve) = (sem(n) for n in (
                "h_in", "g_in", "k_in", "wo_taken", "wq_taken", "d_squares", "d_roots", "d_scales", "xn_done",
                "xn_transposed", "xnT_odd", "xnT_even", "keys_transposed", "keys_out", "scores_done", "scores_odd",
                "scores_even"))
            with nc.Block() as block:
                @block.sync
                def _(sp):
                    load_panels(sp, wout_panel, 2, G_WO)
                    load_panels(sp, wq_panel, 2, G_WQ, 0)
                    load_turn(sp, kvk_panel, 0, G_KK)

                @block.gpsimd
                def _(pool):
                    for m in range(MT):
                        nc.gpsimd.dma_start(h_tok[:, m, :], a["x"][0, m * P:(m + 1) * P, :]).then_inc(h_in, 16)
                    nc.gpsimd.dma_start(grow[:, :], a["norm2_g"][0:1, :].broadcast_to([P, D])).then_inc(g_in, 16)
                    for n, name in enumerate(("peer_k1", "peer_k2")):
                        nc.gpsimd.dma_start(kraw[:, n * PH:(n + 1) * PH, :],
                                            a[name][0].rearrange("h n d -> n h d")).then_inc(k_in, 16)
                    pool.wait_ge(k_in, 32)

                @block.tensor
                def _(pe):
                    pe_token_tiles(pe, 2, G_WO, lambda k, m: mixT[:, k, m * P:(m + 1) * P], wo_taken,
                                   lambda i, t: i * TPI + (t + 1))
                    pe.wait_ge(k_in, 32)
                    pe.wait_ge(wo_taken, 8 + 2 * TPI)
                    for n in range(2 * PH):
                        last = nc.tensor.transpose(PS[:, 4 + n // 4, (n % 4) * P:(n % 4 + 1) * P], kraw[:, n, :], ident[:, :])
                    last.then_inc(kt_tr, 1)
                    pe.wait_ge(xn_done, MT)
                    for k in range(KT):
                        if k >= 4:
                            pe.wait_ge(tr_act if k % 2 else tr_dve, (k - 4) // 2 + 1)
                        for m in range(MT):
                            last = nc.tensor.transpose(PS[:, k % 4, m * P:(m + 1) * P],
                                                       xn_tok[:, m, k * P:(k + 1) * P], ident[:, :])
                        last.then_inc(tr_done, 1)
                    pe.wait_ge(tr_act, KT // 2)
                    pe.wait_ge(tr_dve, KT // 2)
                    pe.wait_ge(kt_out, 1)
                    pe_tiles(pe, 2, G_WQ, lambda k: xnT[:, k, :], TX, wq_taken, lambda i, t: i * TPI + (t + 1))
                    pe.wait_ge(wq_taken, 8 + 2 * TPI)
                    for m in range(MT):
                        for h in range(PH):
                            for side in range(2):
                                last = nc.tensor.matmul(
                                    PS[:, 4 * m + h // 2, (h % 2) * 2 * NKEY + side * NKEY:][:, 0:NKEY],
                                    q2T[:, 2 * h + side, m * P:(m + 1) * P], kT[:, side * PH + h, :],
                                    start=True, stop=True)
                            if h % 2:
                                last.then_inc(sc_done, 1)

                @block.scalar
                def _(act):
                    act.sem_inc(wq_taken, 8)
                    act.wait_ge(wo_taken, 8 + 2 * TPI)
                    for m in range(MT):
                        if m:
                            act.wait_ge(sq_done, m)
                        nc.scalar.activation(ssq[:, :], h_tok[:, m, :], ACT.Square, accum_out=rs2[:, 0, m:m + 1]).then_inc(sq_done, 1)
                    act.wait_ge(sq_done, MT)
                    nc.scalar.activation(rs2[:, 1, :], rs2[:, 0, :], ACT.Sqrt, bias=eps_c[:, :], scale=1.0 / D).then_inc(rt_done, 1)
                    act.wait_ge(kt_tr, 1)
                    nc.scalar.activation(kT[:, :, :], PS[:, 4:8, :].rearrange("p b (t n) -> p (b t) n", n=P),
                                         ACT.Copy).then_inc(kt_out, 1)
                    for k in range(1, KT, 2):
                        act.wait_ge(tr_done, k + 1)
                        nc.scalar.activation(xnT[:, k, :], PS[:, k % 4, 0:TX], ACT.Copy).then_inc(tr_act, 1)
                    with act.Fori(0, 2) as i:
                        for t in range(TPI):
                            act.wait_ge(tile_ready, ready_at(G_WQ, i, t))
                            nc.scalar.activation(q2T[:, ds(i * TPI + t, 1), :], PS[:, t, 0:TX], ACT.Copy).then_inc(wq_taken, 1)
                    for b in range(1, BANKS, 2):
                        act.wait_ge(sc_done, b + 1)
                        nc.scalar.activation(scores[:, 2 * b:2 * b + 2, :], PS[:, b, :].rearrange("p (h n) -> p h n", h=2),
                                             ACT.Copy).then_inc(sc_act, 1)

                @block.vector
                def _(dve):
                    dve.sem_inc(wo_taken, 8)
                    dve.wait_ge(h_in, 32)
                    with dve.Fori(0, 2) as i:
                        for s in range(RING):
                            for m in range(MT):
                                t = s * MT + m
                                dve.wait_ge(tile_ready, ready_at(G_WO, i, t))
                                hc = h_tok[:, m, ds(i * (RING * PW) + s * PW, PW)]
                                nc.vector.tensor_tensor(hc, hc, PS[:, t, 0:PW], ALU.add).then_inc(wo_taken, 1)
                    dve.wait_ge(wo_taken, 8 + 2 * TPI)
                    dve.wait_ge(rt_done, 1)
                    nc.vector.reciprocal(rs2[:, 0, :], rs2[:, 1, :]).then_inc(rs_done, 1)
                    dve.wait_ge(rs_done, 1)
                    dve.wait_ge(g_in, 16)
                    for m in range(MT):
                        nc.vector.scalar_tensor_tensor(xn_tok[:, m, :], h_tok[:, m, :], rs2[:, 0, m:m + 1], grow[:, :],
                                                       ALU.mult, ALU.mult).then_inc(xn_done, 1)
                    for k in range(0, KT, 2):
                        dve.wait_ge(tr_done, k + 1)
                        nc.vector.tensor_copy(xnT[:, k, :], PS[:, k % 4, 0:TX]).then_inc(tr_dve, 1)
                    for b in range(0, BANKS, 2):
                        dve.wait_ge(sc_done, b + 1)
                        nc.vector.tensor_copy(scores[:, 2 * b:2 * b + 2, :],
                                              PS[:, b, :].rearrange("p (h n) -> p h n", h=2)).then_inc(sc_dve, 1)

        US, VS = 4, 4
        HN = MT * PH
        with phase() as c:
            Ug = sb(c, "Ug", [P, US, D])
            Vg = sb(c, "Vg", [P, VS, D])
            diag = flat(mixT)[:, 0:PTOP * P].rearrange("p (j n) -> p j n", n=P)
            top = flat(mixT)[:, PTOP * P:]
            _o = [0]

            def piece(*shape):
                n = 1
                for x in shape:
                    n *= x
                ap = top[:, _o[0]:_o[0] + n]
                _o[0] += n
                if len(shape) == 2:
                    return ap.rearrange("p (a b) -> p a b", b=shape[1])
                if len(shape) == 3:
                    return ap.rearrange("p (a b c) -> p a b c", b=shape[1], c=shape[2])
                return ap

            sw, sw2 = piece(2, NKEY), piece(2, NKEY)
            val, idxf, posf, picked = piece(2, PTOP), piece(2, PTOP), piece(2, PTOP), piece(2, PTOP)
            cand, cand2 = piece(PTOP * PTOP), piece(PTOP * PTOP)
            hot = piece(2, PTOP, PTOP)
            best, negmax, ex, den = piece(2, PTOP), piece(2), piece(2, PTOP), piece(2)
            rden, dots, gel, wgt = piece(1), piece(PTOP), piece(PTOP), piece(PTOP)
            iota = piece(PTOP)
            keyi = sb(c, "keyi", [P, 2, PTOP], U32)
            posi = sb(c, "posi", [P, 3, PTOP], U32)
            idx = sb(c, "idx", [P, 2, PTOP], U32)
            zer = sb(c, "zer", [P, BANK])
            (f_const, found, chain, u_used, v_used, max_ready, exp_ready, dots_ready, gelu_ready, w_ready, diag_ready,
             y_done, y_added, pool_step, dve_step) = (sem(n) for n in (
                "peer_consts", "found", "topk_chain", "u_used", "v_used", "max_ready", "gates_exp", "dots_ready",
                "gelu_ready", "weights_ready", "diag_ready", "y_done", "y_added", "pool_step", "dve_step"))
            u_in = [sem(f"u_in{s}") for s in range(US)]
            v_in = [sem(f"v_in{s}") for s in range(VS)]
            LOWEST = -3.0e38

            def heads(eng, one_head):
                for m in range(MT):
                    pairs = PH // 2 - (m == MT - 1)
                    with eng.Fori(0, pairs) as i:
                        for par in range(2):
                            one_head(i * 2 + (m * PH + par), par, m, True)
                    if m == MT - 1:
                        for par in range(2):
                            one_head(HN - 2 + par, par, m, par == 0)

            with nc.Block() as block:
                @block.sync
                def _(sp):
                    pass

                @block.gpsimd
                def _(pool):
                    nc.gpsimd.iota(iota, [[1, PTOP]], base=0, channel_multiplier=0,
                                   allow_small_or_imprecise_dtypes=True).then_inc(f_const, 1)
                    nc.gpsimd.memset(zer[:, :], 0.0).then_inc(f_const, 1)

                    def one_head(n, par, m, ahead):
                        pool.wait_ge(found, n + 1)
                        for table, slots, used, loaded, buf in ((a["peer_u"][0], US, u_used, u_in, Ug),
                                                                (a["peer_v"][0], VS, v_used, v_in, Vg)):
                            for j in range(PTOP):
                                pool.wait_ge(used, n * PTOP + (j + 1))
                                pool.sem_inc(pool_step, 1)
                                nc.gpsimd.indirect_dma_start(
                                    buf[:, j % slots, :], None, table,
                                    bass.IndirectOffsetOnAxis(ap=idx[:, par, j:j + 1], axis=0)).then_inc(loaded[j % slots], 16)
                    heads(pool, one_head)

                @block.tensor
                def _(pe):
                    pe.sem_inc(v_used, VS)
                    pe.wait_ge(f_const, 2)
                    for b in range(BANKS):
                        nc.tensor.matmul(PS[:, b, :], zer[:, 0:P], zer[:, :], start=True, stop=False)

                    def one_head(n, par, m, ahead):
                        for j in range(PTOP):
                            pe.wait_ge(v_in[j % VS], n * (16 * PTOP // VS) + 16 * (j // VS + 1))
                            pe.wait_ge(diag_ready, n * PTOP + (j + 2))
                            for b in range(D // BANK):
                                last = nc.tensor.matmul(PS[:, 4 * m + b, :], diag[:, j, :],
                                                        Vg[:, j % VS, b * BANK:(b + 1) * BANK], start=False, stop=False)
                            last.then_inc(v_used, 1)
                    heads(pe, one_head)
                    for b in range(BANKS):
                        last = nc.tensor.matmul(PS[:, b, :], zer[:, 0:P], zer[:, :], start=False, stop=True)
                    last.then_inc(y_done, 1)

                @block.scalar
                def _(act):
                    def gates(n, par):
                        act.wait_ge(max_ready, n + 1)
                        nc.scalar.activation(ex[:, par, :], best[:, par, :], ACT.Exp, bias=negmax[:, par:par + 1],
                                             accum_out=den[:, par:par + 1]).then_inc(exp_ready, 1)

                    def one_head(n, par, m, ahead):
                        if ahead:
                            gates(n + 1, 1 - par)
                        act.wait_ge(u_used, n * PTOP + (US + PTOP))
                        nc.scalar.activation(gel, dots, ACT.Gelu).then_inc(gelu_ready, 1)
                        act.wait_ge(w_ready, n + 1)
                        act.wait_ge(v_used, n * PTOP + VS)
                        for j in range(PTOP):
                            nc.scalar.activation(diag[:, j, :], ident[:, :], ACT.Copy, scale=wgt[:, j:j + 1]).then_inc(diag_ready, 1)
                    act.sem_inc(diag_ready, 1)
                    gates(0, 0)
                    heads(act, one_head)

                @block.vector
                def _(dve):
                    dve.sem_inc(u_used, US)
                    dve.wait_ge(f_const, 2)
                    LINKS = 21

                    def search(n, par):
                        at = [0]

                        def link(ins):
                            at[0] += 1
                            ins.then_inc(chain, 1)
                            dve.wait_ge(chain, n * LINKS + at[0])

                        def top16(out, where, src, src2):
                            dve.sem_inc(dve_step, 1)
                            link(nc.vector.max(out[:, 0:8], src))
                            dve.sem_inc(dve_step, 1)
                            nc.vector.max_index(where[:, 0:8], out[:, 0:8], src)
                            link(nc.vector.match_replace(src2, out[:, 0:8], src, LOWEST))
                            dve.sem_inc(dve_step, 1)
                            link(nc.vector.max(out[:, 8:16], src2))
                            dve.sem_inc(dve_step, 1)
                            link(nc.vector.max_index(where[:, 8:16], out[:, 8:16], src2))

                        link(nc.vector.tensor_copy(sw, scores[:, ds(n, 1), :].rearrange("p o (s k) -> p (o s) k", s=2)))
                        for side in range(2):
                            top16(val[:, side, :], keyi[:, side, :], sw[:, side, :], sw2[:, side, :])
                        link(nc.vector.tensor_copy(idxf, keyi[:, :, :]))
                        link(nc.vector.tensor_tensor(cand.rearrange("p (a b) -> p a b", b=PTOP),
                                                     val[:, 0, :].unsqueeze(2).broadcast_to([P, PTOP, PTOP]),
                                                     val[:, 1, :].unsqueeze(1).broadcast_to([P, PTOP, PTOP]), ALU.add))
                        top16(best[:, par, :], posi[:, 0, :], cand, cand2)
                        nc.vector.tensor_scalar(negmax[:, par:par + 1], best[:, par, 0:1], -1.0, None,
                                                ALU.mult).then_inc(max_ready, 1)
                        link(nc.vector.tensor_scalar(posi[:, 1, :], posi[:, 0, :], 4, None, ALU.logical_shift_right))
                        link(nc.vector.tensor_scalar(posi[:, 2, :], posi[:, 0, :], PTOP - 1, None, ALU.bitwise_and))
                        link(nc.vector.tensor_copy(posf, posi[:, 1:3, :]))
                        link(nc.vector.tensor_tensor(hot, posf.unsqueeze(3).broadcast_to([P, 2, PTOP, PTOP]),
                                                     iota.unsqueeze(1).unsqueeze(1).broadcast_to([P, 2, PTOP, PTOP]),
                                                     ALU.is_equal))
                        link(nc.vector.tensor_tensor(hot, hot, idxf.unsqueeze(2).broadcast_to([P, 2, PTOP, PTOP]), ALU.mult))
                        link(nc.vector.tensor_reduce(picked, hot, axis=AX.X, op=ALU.add))
                        assert at[0] == LINKS, at[0]

                    def publish(par, gathered):
                        dve.wait_ge(v_used, gathered * PTOP + VS)
                        nc.vector.scalar_tensor_tensor(idx[:, par, :], picked[:, 0, :], float(NKEY), picked[:, 1, :],
                                                       ALU.mult, ALU.add).then_inc(found, 1)

                    def one_head(n, par, m, ahead):
                        if ahead:
                            search(n + 1, 1 - par)
                            publish(1 - par, n)
                        for j in range(PTOP):
                            dve.wait_ge(u_in[j % US], n * (16 * PTOP // US) + 16 * (j // US + 1))
                            nc.vector.tensor_tensor_reduce(out=Ug[:, j % US, :], in0=Ug[:, j % US, :], in1=xn_tok[:, m, :],
                                                           scale=1.0, scalar=0.0, op0=ALU.mult, op1=ALU.add,
                                                           accum_out=dots[:, j:j + 1]).then_inc(u_used, 1)
                        dve.wait_ge(exp_ready, n + 1)
                        nc.vector.reciprocal(rden, den[:, par:par + 1]).then_inc(dots_ready, 1)
                        dve.wait_ge(dots_ready, n + 1)
                        dve.wait_ge(gelu_ready, n + 1)
                        dve.wait_ge(diag_ready, n * PTOP + 1)
                        nc.vector.scalar_tensor_tensor(wgt, gel, rden, ex[:, par, :], ALU.mult, ALU.mult).then_inc(w_ready, 1)

                    search(0, 0)
                    publish(0, 0)
                    heads(dve, one_head)
                    dve.wait_ge(y_done, 1)
                    nc.vector.tensor_tensor(flat(conv_y), flat(conv_y), PS[:, :, :].rearrange("p b n -> p (b n)"),
                                            ALU.add).then_inc(y_added, 1)

        two = outer.enter_context(ExitStack())
        A2 = sb(two, "A2", [P, 56, TX])
        kx = sb(two, "kx", [P, XH * XD // P, TX])
        vx = sb(two, "vx", [P, MT, XH * XD])
        memT, hT, x1 = mixT, xnT, h_tok
        A2f = flat(A2)
        with phase() as c:
            mem_tok = A2f[:, 0:MT * D].rearrange("p (m n) -> p m n", n=D)
            frow, junk = A2f[:, 2 * D:3 * D], A2f[:, 3 * D:4 * D]
            st = sb(c, "st", [P, 2, 6])
            (m_in, f_in, sq_done, rt_done, rs_done, scaled, tr_done, tr_act, tr_dve) = (sem(n) for n in (
                "mem_in", "normf_in", "g_squares", "g_roots", "g_scales", "g_scaled", "g_transposed", "g_odd", "g_even"))
            with nc.Block() as block:
                @block.sync
                def _(sp):
                    for m in range(MT):
                        sp.dma_start(mem_tok[:, m, :], a["mem_2"][0, m * P:(m + 1) * P, :]).then_inc(m_in, 16)
                    sp.dma_start(frow, a["normf_g"].unsqueeze(0).broadcast_to([P, D])).then_inc(f_in, 16)

                @block.scalar
                def _(act):
                    for n, src in enumerate((h_tok[:, 0, :], h_tok[:, 1, :], mem_tok[:, 0, :], mem_tok[:, 1, :],
                                             x1[:, 0, :], x1[:, 1, :])):
                        if n == 2:
                            act.wait_ge(m_in, 32)
                        if n:
                            act.wait_ge(sq_done, n)
                        if n >= 4:
                            act.wait_ge(scaled, n - 3)
                        nc.scalar.activation(junk, src, ACT.Square, accum_out=st[:, 0, n:n + 1]).then_inc(sq_done, 1)
                        if n % 2:
                            act.wait_ge(sq_done, n + 1)
                            nc.scalar.activation(st[:, 1, n - 1:n + 1], st[:, 0, n - 1:n + 1], ACT.Sqrt, bias=eps_c[:, :],
                                                 scale=1.0 / D).then_inc(rt_done, 1)
                    for k in range(1, 2 * KT, 2):
                        act.wait_ge(tr_done, k + 1)
                        dst, g = (memT, "mem_norm_g_2") if k < KT else (hT, "norm_g_2")
                        nc.scalar.activation(dst[:, k % KT, :], PS[:, k % BANKS, 0:TX], ACT.Copy,
                                             scale=pcol(g, k % KT)).then_inc(tr_act, 1)

                @block.vector
                def _(dve):
                    dve.wait_ge(rt_done, 1)
                    nc.vector.reciprocal(st[:, 0, 0:2], st[:, 1, 0:2]).then_inc(rs_done, 1)
                    dve.wait_ge(rs_done, 1)
                    dve.wait_ge(f_in, 16)
                    for m in range(MT):
                        nc.vector.scalar_tensor_tensor(x1[:, m, :], h_tok[:, m, :], st[:, 0, m:m + 1], frow, ALU.mult,
                                                       ALU.mult).then_inc(scaled, 1)
                    dve.wait_ge(rt_done, 2)
                    nc.vector.reciprocal(st[:, 0, 2:4], st[:, 1, 2:4]).then_inc(rs_done, 1)
                    dve.wait_ge(rs_done, 2)
                    for m in range(MT):
                        nc.vector.tensor_scalar(mem_tok[:, m, :], mem_tok[:, m, :], st[:, 0, 2 + m:3 + m], None,
                                                ALU.mult).then_inc(scaled, 1)
                    dve.wait_ge(rt_done, 3)
                    nc.vector.reciprocal(st[:, 0, 4:6], st[:, 1, 4:6]).then_inc(rs_done, 1)
                    dve.wait_ge(rs_done, 3)
                    for m in range(MT):
                        nc.vector.tensor_scalar(xn_tok[:, m, :], x1[:, m, :], st[:, 0, 4 + m:5 + m], None,
                                                ALU.mult).then_inc(scaled, 1)
                    for k in range(0, 2 * KT, 2):
                        dve.wait_ge(tr_done, k + 1)
                        dst, g = (memT, "mem_norm_g_2") if k < KT else (hT, "norm_g_2")
                        nc.vector.tensor_scalar(dst[:, k % KT, :], PS[:, k % BANKS, 0:TX], pcol(g, k % KT), None,
                                                ALU.mult).then_inc(tr_dve, 1)

                @block.tensor
                def _(pe):
                    for k in range(2 * KT):
                        if k in (0, KT):
                            pe.wait_ge(scaled, 4 if k == 0 else 6)
                        if k >= BANKS:
                            pe.wait_ge(tr_act if k % 2 else tr_dve, (k - BANKS) // 2 + 1)
                        src = mem_tok if k < KT else xn_tok
                        for m in range(MT):
                            last = nc.tensor.transpose(PS[:, k % BANKS, m * P:(m + 1) * P],
                                                       src[:, m, (k % KT) * P:(k % KT + 1) * P], ident[:, :])
                        last.then_inc(tr_done, 1)

        abT = sb(two, "abT", [VH, 2, TX])
        with phase() as c:
            o_flat = flat(oT)
            PD = DCONV - 1
            cin = o_flat[:, 0:4 * (PD + TX)].rearrange("p (s n) -> p s n", n=PD + TX)
            dacc = o_flat[:, 1100:1100 + 4 * TX].rearrange("p (s n) -> p s n", n=TX)
            wab = o_flat[:, 2200:2200 + KT * 2 * VH].rearrange("p (k n) -> p k n", n=2 * VH)
            (ab_in, kk_taken, kv_taken, dn_taken, xq_taken, ab_done, ab_out, pad_done, dchain, silu_done) = (
                sem(n) for n in ("wab_in", "kk_taken", "kv_taken", "dn_taken", "xq_taken", "ab_done", "ab_out",
                                 "dpad_done", "dconv_chain", "silu_done"))
            NQ = CQKV // P // TPI
            with nc.Block() as block:
                @block.sync
                def _(sp):
                    sp.dma_start(wab, w_dn.rearrange("(k p) n -> p k n", p=P)[:, :, C_AB:C_XQ]).then_inc(ab_in, 16)
                    load_turn(sp, kvv_panel, 0, G_KV)
                    load_panels(sp, dqkv_panel, NQ, G_DN, 0)
                    load_turn(sp, xq_panel, 0, G_XQ)

                @block.tensor
                def _(pe):
                    def section(width, moving, taken, g0, turns):
                        pe_tiles(pe, turns, g0, moving, width, taken, lambda i, t: i * TPI + (t + 1))
                        pe.wait_ge(taken, 8 + turns * TPI)
                    section(TX, lambda k: memT[:, k, :], kk_taken, G_KK, 1)
                    pe_token_tiles(pe, 1, G_KV, lambda k, m: memT[:, k, m * P:(m + 1) * P], kv_taken,
                                   lambda i, t: i * TPI + (t + 1))
                    pe.wait_ge(kv_taken, 8 + TPI)
                    section(TX, lambda k: hT[:, k, :], dn_taken, G_DN, NQ)
                    section(TX, lambda k: hT[:, k, :], xq_taken, G_XQ, 1)
                    pe.wait_ge(ab_in, 16)
                    for n in range(2):
                        for k in range(KT):
                            last = nc.tensor.matmul(PS[0:VH, n, 0:TX], wab[:, k, n * VH:(n + 1) * VH], hT[:, k, :],
                                                    start=(k == 0), stop=(k == KT - 1))
                    last.then_inc(ab_done, 1)

                @block.scalar
                def _(act):
                    for taken in (kk_taken, kv_taken, dn_taken, xq_taken):
                        act.sem_inc(taken, 8)
                    for t in range(TPI):
                        act.wait_ge(tile_ready, ready_at(G_KK, 0, t))
                        nc.scalar.activation(kx[:, t, :], PS[:, t, 0:TX], ACT.Copy).then_inc(kk_taken, 1)
                    for t in range(TPI):
                        act.wait_ge(tile_ready, ready_at(G_KV, 0, t))
                        nc.scalar.activation(vx[:, t % MT, (t // MT) * PW:(t // MT + 1) * PW], PS[:, t, 0:PW],
                                             ACT.Copy).then_inc(kv_taken, 1)
                    act.wait_ge(pad_done, 1)
                    act.sem_inc(silu_done, 4)
                    with act.Fori(0, NQ) as i:
                        for t in range(TPI):
                            act.wait_ge(tile_ready, ready_at(G_DN, i, t))
                            act.wait_ge(silu_done, i * TPI + (t + 1))
                            nc.scalar.activation(cin[:, t % 4, PD:], PS[:, t, 0:TX], ACT.Copy).then_inc(dn_taken, 1)
                            if t % 4 == 3:
                                for u in range(t - 3, t + 1):
                                    act.wait_ge(dchain, i * (TPI * DCONV) + DCONV * (u + 1))
                                    nc.scalar.activation(A2[:, ds(i * TPI + u, 1), :], dacc[:, u % 4, :],
                                                         ACT.Silu).then_inc(silu_done, 1)
                    for t in range(TPI):
                        act.wait_ge(tile_ready, ready_at(G_XQ, 0, t))
                        nc.scalar.activation(A2[:, 48 + t, :], PS[:, t, 0:TX], ACT.Copy).then_inc(xq_taken, 1)
                    act.wait_ge(ab_done, 1)
                    nc.scalar.activation(abT[:, :, :], PS[0:VH, 0:2, 0:TX], ACT.Copy).then_inc(ab_out, 1)

                @block.vector
                def _(dve):
                    nc.vector.memset(cin[:, :, 0:PD], 0.0).then_inc(pad_done, 1)
                    with dve.Fori(0, NQ) as i:
                        for t in range(TPI):
                            dve.wait_ge(dn_taken, i * TPI + (8 + t + 1))
                            dve.wait_ge(silu_done, i * TPI + (t // 4 * 4) + 4)
                            for j in range(DCONV):
                                w = dcw[:, ds(i * TPI + (j * (CQKV // P) + t), 1)]
                                src, dst = cin[:, t % 4, j:j + TX], dacc[:, t % 4, :]
                                if j == 0:
                                    ins = nc.vector.tensor_scalar(dst, src, w, None, ALU.mult)
                                else:
                                    dve.wait_ge(dchain, i * (TPI * DCONV) + (DCONV * t + j))
                                    ins = nc.vector.scalar_tensor_tensor(dst, src, w, dst, ALU.mult, ALU.add)
                                ins.then_inc(dchain, 1)

        mix_f = flat(mixT)
        NB_ = 8

        class Norms:

            def __init__(self, jobs, tag, sq, rt):
                self.jobs, self.sq, self.rt = jobs, sq, rt
                self.squares, self.summed, self.roots, self.inverse, self.normed = (
                    sem(tag + n) for n in ("_squares", "_summed", "_roots", "_inverse", "_normed"))
                self.marks = []
                n = 0
                for _, _, _, gain in jobs:
                    n += NB_ if gain else 1
                    self.marks.append(n)

            def bank0(self, n):
                return 4 * (n % 2)

            def scalar(self, act):
                for n, (tiles, per, scale, _) in enumerate(self.jobs):
                    if n >= 2:
                        act.wait_ge(self.summed, n - 1)
                    nc.scalar.activation(self.sq[:, n % 2, :, :], tiles, ACT.Square).then_inc(self.squares, 1)
                    act.wait_ge(self.summed, n + 1)
                    if n >= 2:
                        act.wait_ge(self.normed, self.marks[n - 2])
                    w = NB_ // per
                    nc.scalar.activation(self.rt[:, n % 2, 0:w, :],
                                         PS[:, self.bank0(n):self.bank0(n) + w // 2, :].rearrange(
                                             "p b (t n) -> p (b t) n", n=TX), ACT.Sqrt, bias=eps_c[:, :],
                                         scale=scale).then_inc(self.roots, 1)

            def tensor(self, pe):
                for n, (_, per, _, _) in enumerate(self.jobs):
                    pe.wait_ge(self.squares, n + 1)
                    if n >= 2:
                        pe.wait_ge(self.roots, n - 1)
                    for g in range(NB_ // per):
                        for e in range(per):
                            last = nc.tensor.matmul(PS[:, self.bank0(n) + g // 2, (g % 2) * TX:(g % 2 + 1) * TX],
                                                    ones[:, :], self.sq[:, n % 2, g * per + e, :], start=(e == 0),
                                                    stop=(e == per - 1))
                    last.then_inc(self.summed, 1)

            def vector(self, dve):
                for n, (tiles, per, _, gain) in enumerate(self.jobs):
                    dve.wait_ge(self.roots, n + 1)
                    w = NB_ // per
                    r = self.rt[:, n % 2, 0:w, :]
                    nc.vector.reciprocal(r, r).then_inc(self.inverse, 1)
                    dve.wait_ge(self.inverse, n + 1)
                    if gain is None:
                        nc.vector.tensor_tensor(tiles, tiles, r, ALU.mult).then_inc(self.normed, 1)
                    else:
                        for t in range(NB_):
                            nc.vector.scalar_tensor_tensor(tiles[:, t, :], tiles[:, t, :], gain(t), r[:, t // per, :],
                                                           ALU.mult, ALU.mult).then_inc(self.normed, 1)

        def step_tiles(ap, at):
            return ap[:, at:at + NB_, :]

        VG = 4
        NG = VH // VG
        QG = VG * KH // VH
        rest = flat(xT)[:, KT * TX:KT * T]
        gcT = abT[:, 0, :]
        NCOL = 3 * MT * VH
        col = rest[:, 0:NCOL].rearrange("p (a m h) -> p a m h", a=3, m=MT)
        hlog = rest[0:VH, NCOL:NCOL + 3]
        LEV = 7
        x_f, o_f = ring[:, :, :, :].rearrange("p s k n -> p (s k n)"), flat(oT)
        lev = x_f[:, 2816:2816 + LEV * P].rearrange("p (l n) -> p l n", n=P)
        mneg = x_f[:, 2816 + LEV * P:2816 + (LEV + 1) * P]
        with phase() as c:
            sqj = mix_f[:, 0:2 * NB_ * TX].rearrange("p (s t n) -> p s t n", s=2, n=TX)
            rtj = o_f[:, 0:2 * NB_ * TX].rearrange("p (s t n) -> p s t n", s=2, n=TX)
            norms = Norms([(step_tiles(A2, 0), 1, 1.0, None), (step_tiles(A2, 8), 1, 1.0, None),
                           (step_tiles(A2, 16), 1, 1.0, None),
                           (step_tiles(A2, 48), 2, 1.0 / XD, lambda t: pcol("xa_q_norm_g_2", t % 2)),
                           (step_tiles(kx, 0), 2, 1.0 / XD, lambda t: pcol("xa_k_norm_g_2", t % 2))],
                          "qk", sqj, rtj)
            bchain, gchain, dchain2, hin, mchain, ttr, tout = (sem(n) for n in (
                "beta_chain", "decay_ready", "decay_chain", "hlog_in", "level_masks", "cols_transposed", "cols_out"))
            tmpa = x_f[0:VH, 0:TX]
            keep2 = x_f[0:VH, TX:2 * TX]
            with nc.Block() as block:
                @block.sync
                def _(sp):
                    sp.dma_start(hlog[:, 0:1], a["dn_a_log_2"].rearrange("o h -> h o")).then_inc(hin, 16)
                    sp.dma_start(hlog[:, 1:2], a["dn_dt_bias_2"].rearrange("o h -> h o")).then_inc(hin, 16)
                    sp.wait_ge(hin, 32)

                @block.gpsimd
                def _(pool):
                    at = [0]

                    def link(ins):
                        at[0] += 1
                        ins.then_inc(mchain, 1)
                        pool.wait_ge(mchain, at[0])
                    link(nc.gpsimd.memset(keep2, 1.0))
                    link(nc.gpsimd.memset(keep2.rearrange("p (c n) -> p c n", n=P)[:, :, 0:1], 0.0))
                    link(nc.gpsimd.memset(mneg, 0.0))
                    link(nc.gpsimd.affine_select(out=mneg, in_=mneg, compare_op=ALU.is_ge, fill=-30000.0, base=0,
                                                 pattern=[[1, P]], channel_multiplier=-1))
                    for l in range(LEV):
                        half = 1 << l
                        m = lev[:, l, :].rearrange("p (b n) -> p b n", n=2 * half)
                        link(nc.gpsimd.memset(lev[:, l, :], 1.0))
                        link(nc.gpsimd.memset(m[:, :, 0:half], 0.0))
                        link(nc.gpsimd.affine_select(out=m, in_=m, compare_op=ALU.is_ge, fill=0.0, base=0,
                                                     pattern=[[-2 * half, P // (2 * half)], [0, 2 * half]],
                                                     channel_multiplier=1))
                        link(nc.gpsimd.affine_select(out=m, in_=m, compare_op=ALU.is_ge, fill=0.0, base=half - 1,
                                                     pattern=[[2 * half, P // (2 * half)], [0, 2 * half]],
                                                     channel_multiplier=-1))

                @block.tensor
                def _(pe):
                    norms.tensor(pe)
                    pe.wait_ge(norms.roots, 5)
                    pe.wait_ge(gchain, 1)
                    pe.wait_ge(bchain, 6)
                    for m in range(MT):
                        nc.tensor.transpose(PS[:, 0, m * VH:(m + 1) * VH], gcT[:, m * P:(m + 1) * P], ident[0:VH, 0:VH])
                        last = nc.tensor.transpose(PS[:, 0, (MT + m) * VH:(MT + m + 1) * VH],
                                                   abT[:, 1, m * P:(m + 1) * P], ident[0:VH, 0:VH])
                    last.then_inc(ttr, 1)

                @block.scalar
                def _(act):
                    norms.scalar(act)
                    act.wait_ge(hin, 32)
                    nc.scalar.activation(abT[:, 0, :], abT[:, 0, :], ACT.Identity, bias=hlog[:, 1:2]).then_inc(bchain, 1)
                    act.wait_ge(bchain, 1)
                    nc.scalar.activation(tmpa, abT[:, 0, :], ACT.Abs).then_inc(bchain, 1)
                    act.wait_ge(bchain, 2)
                    nc.scalar.activation(tmpa, tmpa, ACT.Exp, scale=-1.0).then_inc(bchain, 1)
                    act.wait_ge(bchain, 3)
                    nc.scalar.activation(tmpa, tmpa, ACT.Ln, bias=1.0).then_inc(bchain, 1)
                    nc.scalar.activation(hlog[:, 2:3], hlog[:, 0:1], ACT.Exp).then_inc(bchain, 1)
                    nc.scalar.activation(abT[:, 1, :], abT[:, 1, :], ACT.Sigmoid).then_inc(bchain, 1)
                    act.wait_ge(ttr, 1)
                    nc.scalar.activation(col[:, 0:2, :, :], PS[:, 0, 0:2 * MT * VH].rearrange(
                        "p (a m h) -> p a m h", a=2, m=MT), ACT.Copy).then_inc(tout, 1)
                    act.wait_ge(tout, 1)
                    nc.scalar.activation(col[:, 2, :, :], col[:, 0, :, :], ACT.Exp).then_inc(tout, 1)

                @block.vector
                def _(dve):
                    norms.vector(dve)
                    dve.wait_ge(bchain, 6)
                    dve.wait_ge(mchain, 2)
                    link = []

                    def step(ins):
                        link.append(1)
                        ins.then_inc(dchain2, 1)
                        dve.wait_ge(dchain2, len(link))
                    step(nc.vector.scalar_tensor_tensor(tmpa, abT[:, 0, :], 0.0, tmpa, ALU.max, ALU.add))
                    step(nc.vector.tensor_scalar(tmpa, tmpa, hlog[:, 2:3], -1.0, ALU.mult, ALU.mult))
                    nc.vector.tensor_tensor_scan(gcT, keep2, tmpa, 0.0, ALU.mult, ALU.add).then_inc(gchain, 1)

        with phase() as c:
            def quad(base, at):
                return base[:, at * 1024:(at + 1) * 1024].rearrange("p (m h n) -> p m h n", m=MT, n=P)

            Y, YT, NT_, dT = (quad(o_f, n) for n in range(4))
            att, Pb, u = (quad(mix_f, n) for n in range(3))
            kq = mix_f[:, 3072:4096].rearrange("p (t n) -> p t n", n=TX)
            vg = x_f[:, 0:1024].rearrange("p (h n) -> p h n", n=TX)
            S1 = x_f[:, 1024:1536].rearrange("p (h n) -> p h n", n=P)
            qd = x_f[:, 1536:2048].rearrange("p (h n) -> p h n", n=P)
            ukd = x_f[:, 2048:2560].rearrange("p (h n) -> p h n", n=P)
            kt = x_f[:, 2560:2816].rearrange("p (h n) -> p h n", n=P)
            gsel = u[0:VH, :, :, :].rearrange("p m h n -> p (m h n)").rearrange("p (h n) -> p h n", n=TX)
            No, vt = dT, Pb
            kdl = rest[:, NCOL + 4:NCOL + 4 + VG].rearrange("p (h o) -> p h o", o=1)
            (copied, sel_ready, rows_done, kqk_done, d_ready, dec_ready, qx_ready, n_ready, no_ready, p_done, p_out,
             y_done, y_out, tr_done, vt_out, u_done, u_out, s_done, s1_out, r_ready, ks_done, o_done, o_out,
             kd_ready, fixed, act_step) = (
                sem(n) for n in ("dn_copied", "sel_ready", "rows_done", "kqk_done", "d_ready", "dec_ready", "qx_ready",
                                 "n_ready", "no_ready", "p_done", "p_out", "inv_done", "inv_out", "vk_transposed",
                                 "vk_out", "u_done", "u_out", "s1_done", "s1_out", "r_ready", "ks_done", "do_done",
                                 "do_out", "kd_ready", "fixed", "act_step"))
            SC = DH ** -0.5

            def q4(bank):
                return PS[:, bank, :].rearrange("p (h n) -> p h n", n=P)

            def cast4(x):
                return x.broadcast_to([P, VG, P])

            def colg(which, m, i):
                return col[:, which, m, ds(i * VG, VG)].unsqueeze(2)

            def pair(x):
                return x.unsqueeze(2).broadcast_to([P, QG, VG // QG, P])

            def by_pair(x):
                return x.rearrange("p (a b) n -> p a b n", b=VG // QG)

            with nc.Block() as block:
                @block.tensor
                def _(pe):
                    pe.sem_inc(o_done, 1)
                    with pe.Fori(0, NG) as i:
                        pe.wait_ge(sel_ready, i + 1)
                        pe.wait_ge(o_out, i * 2 + 1)
                        for m in range(MT):
                            nc.tensor.matmul(PS[:, m, :], ones[0:VH, :], gsel[:, :, m * P:(m + 1) * P],
                                             start=True, stop=True).then_inc(rows_done, 1)
                        pe.wait_ge(copied, i * 3 + 3)
                        for m in range(MT):
                            tok = slice(m * P, (m + 1) * P)
                            for w in range(2 * QG):
                                last = nc.tensor.matmul(PS[:, 2 + m, w * P:(w + 1) * P], kq[:, w % QG, tok],
                                                        kq[:, w, tok], start=True, stop=True)
                            last.then_inc(kqk_done, 1)
                        for l in range(LEV):
                            for m in range(MT):
                                pe.wait_ge(no_ready, i * (LEV * MT) + (l * MT + m + 1))
                                if l:
                                    pe.wait_ge(y_out, i * (LEV * MT) + ((l - 1) * MT + m + 1))
                                for h in range(VG):
                                    rhs = ident[:, :] if l == 0 else Y[:, m, h, :]
                                    last = nc.tensor.matmul(PS[:, 4 + m, h * P:(h + 1) * P], No[:, m, h, :], rhs,
                                                            start=True, stop=True)
                                last.then_inc(p_done, 1)
                            if l:
                                for m in range(MT):
                                    pe.wait_ge(p_out, i * (LEV * MT) + (l * MT + m + 1))
                                    for h in range(VG):
                                        last = nc.tensor.matmul(PS[:, 6 + m, h * P:(h + 1) * P], Pb[:, m, h, :],
                                                                YT[:, m, h, :], start=True, stop=True)
                                    if l < LEV - 1:
                                        for h in range(VG):
                                            last = nc.tensor.matmul(PS[:, 2 + m, h * P:(h + 1) * P],
                                                                    YT[:, m, h, :], Pb[:, m, h, :],
                                                                    start=True, stop=True)
                                    last.then_inc(y_done, 1)
                        for m in range(MT):
                            for h in range(VG):
                                last = nc.tensor.transpose(PS[:, m, h * P:(h + 1) * P], vg[:, h, m * P:(m + 1) * P],
                                                           ident[:, :])
                            if m == 0:
                                for w in range(QG):
                                    last = nc.tensor.transpose(PS[:, 2, w * P:(w + 1) * P], kq[:, w, 0:P], ident[:, :])
                            last.then_inc(tr_done, 1)
                        pe.wait_ge(vt_out, i * 3 + 3)
                        pe.wait_ge(y_out, i * (LEV * MT) + LEV * MT)
                        for h in range(VG):
                            last = nc.tensor.matmul(PS[:, 4, h * P:(h + 1) * P], YT[:, 0, h, :], vt[:, 0, h, :],
                                                    start=True, stop=True)
                        last.then_inc(u_done, 1)
                        pe.wait_ge(kd_ready, i + 1)
                        for h in range(VG):
                            last = nc.tensor.matmul(PS[:, 5, h * P:(h + 1) * P], kt[:, h // QG, :], ukd[:, h, :],
                                                    start=True, stop=True)
                        last.then_inc(s_done, 1)
                        pe.wait_ge(s1_out, i + 1)
                        for h in range(VG):
                            last = nc.tensor.matmul(PS[:, 6, h * P:(h + 1) * P], kq[:, h // QG, P:2 * P], S1[:, h, :],
                                                    start=True, stop=True)
                        last.then_inc(ks_done, 1)
                        for h in range(VG):
                            last = nc.tensor.matmul(PS[:, 0, h * P:(h + 1) * P], u[:, 0, h, :], att[:, 0, h, :],
                                                    start=True, stop=True)
                        last.then_inc(o_done, 1)
                        pe.wait_ge(r_ready, i * 2 + 2)
                        for h in range(VG):
                            last = nc.tensor.matmul(PS[:, 7, h * P:(h + 1) * P], YT[:, 1, h, :], vt[:, 1, h, :],
                                                    start=True, stop=True)
                        last.then_inc(u_done, 1)
                        pe.wait_ge(u_out, i * 2 + 2)
                        for h in range(VG):
                            nc.tensor.matmul(PS[:, 1, h * P:(h + 1) * P], S1[:, h, :], qd[:, h, :], start=True,
                                             stop=False)
                            last = nc.tensor.matmul(PS[:, 1, h * P:(h + 1) * P], u[:, 1, h, :], att[:, 1, h, :],
                                                    start=False, stop=True)
                        last.then_inc(o_done, 1)

                @block.scalar
                def _(act):
                    act.sem_inc(o_out, 1)
                    with act.Fori(0, NG) as i:
                        act.wait_ge(o_done, i * 2 + 1)
                        nc.scalar.activation(kq[:, 0:QG, :], A2[:, ds(i * QG + KH, QG), :], ACT.Copy).then_inc(copied, 1)
                        nc.scalar.activation(kq[:, QG:2 * QG, :], A2[:, ds(i * QG, QG), :], ACT.Copy).then_inc(copied, 1)
                        nc.scalar.activation(vg[:, :, :], A2[:, ds(i * VG + 2 * KH, VG), :], ACT.Copy).then_inc(copied, 1)
                        for m in range(MT):
                            act.wait_ge(d_ready, i * 5 + (2 * m + 2))
                            nc.scalar.activation(dT[:, m, :, :], dT[:, m, :, :], ACT.Exp).then_inc(dec_ready, 1)
                        act.wait_ge(d_ready, i * 5 + 5)
                        nc.scalar.activation(kdl[:, :, :], kdl[:, :, :], ACT.Exp).then_inc(dec_ready, 1)
                        nc.scalar.activation(qd, q4(1), ACT.Exp).then_inc(dec_ready, 1)
                        for l in range(LEV):
                            for m in range(MT):
                                act.wait_ge(p_done, i * (LEV * MT) + (l * MT + m + 1))
                                nc.scalar.activation(Pb[:, m, :, :], q4(4 + m), ACT.Copy).then_inc(p_out, 1)
                        act.wait_ge(tr_done, i * 2 + 1)
                        nc.scalar.activation(kt, PS[:, 2, 0:QG * P].rearrange("p (h n) -> p h n", n=P), ACT.Copy).then_inc(vt_out, 1)
                        act.wait_ge(y_out, i * (LEV * MT) + LEV * MT)
                        nc.scalar.activation(vt[:, 0, :, :], q4(0), ACT.Copy).then_inc(vt_out, 1)
                        act.wait_ge(tr_done, i * 2 + 2)
                        nc.scalar.activation(vt[:, 1, :, :], q4(1), ACT.Copy).then_inc(vt_out, 1)
                        act.wait_ge(s_done, i + 1)
                        nc.scalar.activation(S1, q4(5), ACT.Copy).then_inc(s1_out, 1)
                        for m in range(MT):
                            act.wait_ge(o_done, i * 2 + (m + 2))
                            act.sem_inc(act_step, 1)
                            nc.scalar.activation(A2[:, ds(i * VG + 2 * KH, VG), m * P:(m + 1) * P], q4(m), ACT.Copy).then_inc(o_out, 1)

                @block.gpsimd
                def _(pool):
                    with pool.Fori(0, NG) as i:
                        for l in range(LEV):
                            for m in range(MT):
                                if l == 0:
                                    pool.wait_ge(n_ready, i * 6 + (3 * m + 3))
                                else:
                                    pool.wait_ge(p_done, i * (LEV * MT) + ((l - 1) * MT + m + 1))
                                    if l == 1:
                                        pool.wait_ge(y_out, i * (LEV * MT) + (m + 1))
                                nc.gpsimd.tensor_tensor(No[:, m, :, :], NT_[:, m, :, :],
                                                        lev[:, l:l + 1, :].broadcast_to([P, VG, P]), ALU.mult).then_inc(no_ready, 1)

                @block.vector
                def _(dve):
                    with dve.Fori(0, NG) as i:
                        dve.wait_ge(o_done, i * 2 + 1)
                        nc.vector.tensor_tensor(gsel, gcT.unsqueeze(1).broadcast_to([VH, VG, TX]),
                                                ident[0:VH, ds(i * VG, VG)].unsqueeze(2).broadcast_to([VH, VG, TX]),
                                                ALU.mult).then_inc(sel_ready, 1)
                        for m in range(MT):
                            dve.wait_ge(rows_done, i * 2 + (m + 1))
                            nc.vector.tensor_tensor(dT[:, m, :, :], q4(m), cast4(colg(0, m, i)), ALU.subtract).then_inc(d_ready, 1)
                            dve.wait_ge(d_ready, i * 5 + (2 * m + 1))
                            nc.vector.scalar_tensor_tensor(dT[:, m, :, :], dT[:, m, :, :], 0.0,
                                                           mneg.unsqueeze(1).broadcast_to([P, VG, P]), ALU.min,
                                                           ALU.add).then_inc(d_ready, 1)
                        nc.vector.tensor_tensor(kdl[:, :, :], q4(0)[:, :, P - 1:P], colg(0, 0, i), ALU.subtract).then_inc(d_ready, 1)
                        for m in range(MT):
                            dve.wait_ge(dec_ready, i * 4 + (m + 1))
                            dve.wait_ge(kqk_done, i * 2 + (m + 1))
                            kk, qk = q4(2 + m)[:, 0:QG, :], q4(2 + m)[:, QG:2 * QG, :]
                            nc.vector.tensor_tensor(by_pair(NT_[:, m, :, :]), pair(kk), by_pair(dT[:, m, :, :]),
                                                    ALU.mult).then_inc(n_ready, 1)
                            nc.vector.tensor_tensor(by_pair(att[:, m, :, :]), pair(qk), by_pair(dT[:, m, :, :]),
                                                    ALU.mult).then_inc(n_ready, 1)
                            dve.wait_ge(n_ready, i * 6 + (3 * m + 2))
                            nc.vector.tensor_tensor(NT_[:, m, :, :], NT_[:, m, :, :], cast4(colg(1, m, i)),
                                                    ALU.mult).then_inc(n_ready, 1)
                        idb = ident[:, :].unsqueeze(1).broadcast_to([P, VG, P])
                        for m in range(MT):
                            dve.wait_ge(p_done, i * (LEV * MT) + (m + 1))
                            nc.vector.tensor_tensor(YT[:, m, :, :], idb, No[:, m, :, :], ALU.subtract).then_inc(fixed, 1)
                            dve.wait_ge(p_out, i * (LEV * MT) + (m + 1))
                            nc.vector.tensor_tensor(Y[:, m, :, :], idb, Pb[:, m, :, :], ALU.subtract).then_inc(y_out, 1)
                        dve.wait_ge(dec_ready, i * 4 + 4)
                        for w in range(QG):
                            per = VG // QG
                            nc.vector.scalar_tensor_tensor(qd[:, w * per:(w + 1) * per, :], qd[:, w * per:(w + 1) * per, :],
                                                           SC, kq[:, QG + w:QG + w + 1, P:2 * P].broadcast_to([P, per, P]),
                                                           ALU.mult, ALU.mult).then_inc(qx_ready, 1)
                        for m in range(MT):
                            nc.vector.tensor_scalar(att[:, m, :, :], att[:, m, :, :], SC, None, ALU.mult).then_inc(qx_ready, 1)
                        for l in range(1, LEV):
                            for m in range(MT):
                                dve.wait_ge(y_done, i * ((LEV - 1) * MT) + ((l - 1) * MT + m + 1))
                                ins = nc.vector.tensor_tensor(YT[:, m, :, :], YT[:, m, :, :], q4(6 + m), ALU.subtract)
                                if l < LEV - 1:
                                    ins = nc.vector.tensor_tensor(Y[:, m, :, :], Y[:, m, :, :], q4(2 + m), ALU.subtract)
                                ins.then_inc(y_out, 1)
                        dve.wait_ge(u_done, i * 2 + 1)
                        nc.vector.tensor_tensor(u[:, 0, :, :], q4(4), cast4(colg(1, 0, i)), ALU.mult).then_inc(u_out, 1)
                        dve.wait_ge(u_out, i * 2 + 1)
                        nc.vector.tensor_tensor(ukd, u[:, 0, :, :], cast4(kdl[:, :, :]), ALU.mult).then_inc(kd_ready, 1)
                        dve.wait_ge(ks_done, i + 1)
                        dve.wait_ge(vt_out, i * 3 + 3)
                        nc.vector.tensor_tensor(u[:, 1, :, :], q4(6), cast4(colg(2, 1, i)), ALU.mult).then_inc(r_ready, 1)
                        dve.wait_ge(r_ready, i * 2 + 1)
                        nc.vector.tensor_tensor(vt[:, 1, :, :], vt[:, 1, :, :], u[:, 1, :, :], ALU.subtract).then_inc(r_ready, 1)
                        dve.wait_ge(u_done, i * 2 + 2)
                        nc.vector.tensor_tensor(u[:, 1, :, :], q4(7), cast4(colg(1, 1, i)), ALU.mult).then_inc(u_out, 1)

        with phase() as c:
            norms2 = Norms([(step_tiles(A2, 24 + 8 * n), 1, 1.0 / DH, lambda t: pcol("dn_out_norm_g_2", 0))
                            for n in range(3)], "out", sqj, rtj)
            xs = x_f[:, 0:2048].rearrange("p (n m) -> p n m", m=TX)
            pT = x_f[:, 2048:4096].rearrange("p (n m) -> p n m", m=TX)
            red = rest[:, NCOL + 16:NCOL + 16 + 3 * XH * MT].rearrange("p (a n) -> p a n", a=3)
            (s_done, mx, e_done, rcp, p_ready, pt_done, pt_out, xo_done, xo_out) = (sem(n) for n in (
                "xscores_done", "xmax", "xexp", "xrcp", "xp_ready", "xp_transposed", "xpT_out", "xo_done", "xo_out"))
            XS = XD ** -0.5
            with nc.Block() as block:
                @block.tensor
                def _(pe):
                    norms2.tensor(pe)
                    pe.wait_ge(norms2.roots, 3)
                    for h in range(XH):
                        for m in range(MT):
                            for d in range(2):
                                last = nc.tensor.matmul(PS[:, h, m * TX:(m + 1) * TX],
                                                        A2[:, 48 + 2 * h + d, m * P:(m + 1) * P], kx[:, 2 * h + d, :],
                                                        start=(d == 0), stop=(d == 1))
                        last.then_inc(s_done, 1)
                    for h in range(XH):
                        pe.wait_ge(p_ready, MT * (h + 1))
                        if h >= 2:
                            pe.wait_ge(pt_out, h - 1)
                        for m in range(MT):
                            for j in range(MT):
                                last = nc.tensor.transpose(PS[:, 4 + h % 2, j * TX + m * P:j * TX + (m + 1) * P],
                                                           xs[:, MT * h + m, j * P:(j + 1) * P], ident[:, :])
                        last.then_inc(pt_done, 1)
                        pe.wait_ge(pt_out, h + 1)
                        if h >= 2:
                            pe.wait_ge(xo_out, h - 1)
                        for d in range(2):
                            for j in range(MT):
                                last = nc.tensor.matmul(PS[:, 6 + h % 2, d * TX:(d + 1) * TX],
                                                        vx[:, j, (2 * h + d) * P:(2 * h + d + 1) * P],
                                                        pT[:, MT * (h % 4) + j, :], start=(j == 0), stop=(j == MT - 1))
                        last.then_inc(xo_done, 1)

                @block.scalar
                def _(act):
                    norms2.scalar(act)
                    for h in range(XH):
                        for m in range(MT):
                            n = MT * h + m
                            act.wait_ge(mx, 2 * MT * (h + 1))
                            nc.scalar.activation(xs[:, n, :], PS[:, h, m * TX:(m + 1) * TX], ACT.Exp,
                                                 bias=red[:, 1, n:n + 1], scale=XS, accum_out=red[:, 2, n:n + 1]).then_inc(e_done, 1)
                    for h in range(XH):
                        act.wait_ge(pt_done, h + 1)
                        nc.scalar.activation(pT[:, MT * h:MT * (h + 1), :],
                                             PS[:, 4 + h % 2, :].rearrange("p (j n) -> p j n", n=TX), ACT.Copy).then_inc(pt_out, 1)
                        act.wait_ge(xo_done, h + 1)
                        nc.scalar.activation(A2[:, 48 + 2 * h:50 + 2 * h, :],
                                             PS[:, 6 + h % 2, :].rearrange("p (d n) -> p d n", n=TX), ACT.Copy).then_inc(xo_out, 1)

                @block.vector
                def _(dve):
                    norms2.vector(dve)
                    for n in range(XH * MT):
                        dve.wait_ge(s_done, n // MT + 1)
                        nc.vector.reduce_max(red[:, 0, n:n + 1], PS[:, n // MT, (n % MT) * TX:(n % MT + 1) * TX],
                                             AX.X).then_inc(mx, 1)
                        dve.wait_ge(mx, 2 * n + 1)
                        nc.vector.tensor_scalar(red[:, 1, n:n + 1], red[:, 0, n:n + 1], -XS, None, ALU.mult).then_inc(mx, 1)
                    for n in range(XH * MT):
                        dve.wait_ge(e_done, n + 1)
                        nc.vector.reciprocal(red[:, 0, n:n + 1], red[:, 2, n:n + 1]).then_inc(rcp, 1)
                        dve.wait_ge(rcp, n + 1)
                        nc.vector.tensor_scalar(xs[:, n, :], xs[:, n, :], red[:, 0, n:n + 1], None, ALU.mult).then_inc(p_ready, 1)

        with phase() as c:
            zt = o_f[:, 0:4 * TX].rearrange("p (s n) -> p s n", n=TX)
            z_ready, z_taken, g_ready, o2_taken, stored = (sem(n) for n in (
                "zsilu_ready", "zbank_taken", "gated", "o2_taken", "stored"))
            with nc.Block() as block:
                @block.sync
                def _(sp):
                    load_panels(sp, z_panel, 4, G_Z, 0)
                    load_panels(sp, out2_panel, 4, G_O2, 0)
                    sp.wait_ge(o2_taken, 4 + 4 * 4)
                    for m in range(MT):
                        sp.dma_start(out[0, m * P:(m + 1) * P, :], x1[:, m, :]).then_inc(stored, 16)
                    sp.wait_ge(stored, 32)

                @block.tensor
                def _(pe):
                    pe_tiles(pe, 4, G_Z, lambda k: hT[:, k, :], TX, z_ready, lambda i, t: i * TPI + (t + 1))
                    pe.wait_ge(g_ready, 4 + 32)
                    pe.wait_ge(z_ready, 8 + 32)
                    with pe.Fori(0, 4) as i:
                        for cg in range(2):
                            for f in range(2):
                                s = 2 * cg + f
                                pe.wait_ge(slot_loaded[s], 16 * (G_O2 // RING + 1) + i * 16)
                                for m in range(MT):
                                    t = cg * MT + m
                                    if f == 0:
                                        pe.wait_ge(o2_taken, i * 4 + (t + 1))
                                    for k in range(KT):
                                        last = nc.tensor.matmul(PS[:, t, 0:PW], A2[:, 24 + f * KT + k, m * P:(m + 1) * P],
                                                                ring[:, s, k, :], start=(f == 0 and k == 0),
                                                                stop=(f == 1 and k == KT - 1))
                                    last.then_inc(tile_ready, 1)

                @block.scalar
                def _(act):
                    act.sem_inc(z_ready, 8)
                    with act.Fori(0, 4) as i:
                        for t in range(TPI):
                            act.wait_ge(tile_ready, ready_at(G_Z, i, t))
                            act.wait_ge(g_ready, i * TPI + (t + 1))
                            nc.scalar.activation(zt[:, t % 4, :], PS[:, t, 0:TX], ACT.Silu).then_inc(z_ready, 1)

                @block.vector
                def _(dve):
                    dve.sem_inc(o2_taken, 4)
                    dve.sem_inc(g_ready, 4)
                    with dve.Fori(0, 4) as i:
                        for t in range(TPI):
                            dve.wait_ge(z_ready, i * TPI + (8 + t + 1))
                            y = A2[:, ds(i * TPI + (24 + t), 1), :]
                            nc.vector.tensor_tensor(y, y, zt[:, t % 4:t % 4 + 1, :], ALU.mult).then_inc(g_ready, 1)
                    with dve.Fori(0, 4) as i:
                        for cg in range(2):
                            for m in range(MT):
                                dve.wait_ge(tile_ready, i * TPI + (TPI + TPP * G_O2 + 4 * cg + 2 + m + 1))
                                xc = x1[:, m, ds(i * (2 * PW) + cg * PW, PW)]
                                nc.vector.tensor_tensor(xc, xc, PS[:, cg * MT + m, 0:PW], ALU.add).then_inc(o2_taken, 1)


_NAMES = ['x', 'meta_tokens', 'norm1_g', 'w_in', 'w_alpha2', 'b_alpha', 'conv_w', 'conv_b', 'conv_ln_g',
          'conv_ln_b', 'w_conv_out', 'gla_norm_g', 'w_gla_out', 'w_out', 'norm2_g', 'peer_wq', 'peer_k1',
          'peer_k2', 'peer_u', 'peer_v', 'normf_g', 'mem_2', 'norm_g_2', 'mem_norm_g_2', 'mem_w_kv_2',
          'xa_q_norm_g_2', 'xa_k_norm_g_2', 'w_out_2', 'dn_w_in_2', 'dn_conv_w_2', 'dn_a_log_2',
          'dn_dt_bias_2', 'dn_out_norm_g_2']


def kernel(**inputs):
    import numpy as np
    import concourse.bacc as bacc
    from concourse.bass_utils import run_bass_kernel_spmd

    nc = bacc.Bacc("TRN2", target_bir_lowering=False, num_devices=1)
    arrays, a = {}, {}
    for name in _NAMES:
        v = np.ascontiguousarray(inputs[name])
        arrays[f"in_{name}"] = v
        a[name] = nc.dram_tensor(f"in_{name}", v.shape, mybir.dt.from_np(v.dtype), kind="ExternalInput").ap()
    out = nc.dram_tensor("out", (1, TX, D), F32, kind="ExternalOutput").ap()
    build(nc, a, out)
    r = run_bass_kernel_spmd(nc, [arrays], core_ids=[0])
    return r.results[0]["out"]
```
